# Optimizing a Trainium2 kernel written in Bass

```python
import math
import jax, jax.numpy as jnp
from jax import lax
import numpy as np

D_MODEL = 1024
BATCH = 1
SEQ = 256
DEPTH = 4

N_MIXERS = 3
N_SSD = (DEPTH + 2) // 3
N_SC = (DEPTH + 1) // 3
N_NA = DEPTH // 3

SSD_EXPAND = 2
SSD_D_INNER = SSD_EXPAND * D_MODEL
SSD_HEAD_DIM = 64
SSD_HEADS = SSD_D_INNER // SSD_HEAD_DIM
SSD_GROUPS = 8
SSD_STATE = 128
SSD_CONV = 5
SSD_CHUNK = 128
SSD_CONV_DIM = SSD_D_INNER + 2 * SSD_GROUPS * SSD_STATE
SSD_IN_DIM = SSD_D_INNER + SSD_CONV_DIM + 2 * SSD_HEADS
DT_MIN = 1e-3
DT_MAX = 1e-1

SC_CONV = 3

GRID_W = 64
NA_HEADS = 16
NA_HEAD_DIM = D_MODEL // NA_HEADS
NA_WIN_ROWS = 8
NA_WIN_COLS = 16
NA_QCOL_BLOCK = 16
NA_KEY_COLS = NA_QCOL_BLOCK + NA_WIN_COLS

FFN_DIM = 4 * D_MODEL

EPS = 1e-5

kernel_name = 'hybrid_ssd_shortconv_natten_encoder'

def layer_norm(x, g, b):
    xf = x.astype(jnp.float32)
    mu = jnp.mean(xf, axis=-1, keepdims=True)
    var = jnp.mean(jnp.square(xf - mu), axis=-1, keepdims=True)
    y = (xf - mu) * lax.rsqrt(var + EPS)
    return y.astype(x.dtype) * g + b

def grouped_rmsnorm(y, w):
    shp = y.shape
    yg = y.reshape(shp[:-1] + (SSD_GROUPS, shp[-1] // SSD_GROUPS)).astype(jnp.float32)
    yg = yg * lax.rsqrt(jnp.mean(jnp.square(yg), axis=-1, keepdims=True) + EPS)
    return yg.reshape(shp).astype(y.dtype) * w

def depthwise_conv(x, w):
    k = w.shape[0]
    return lax.conv_general_dilated(
        x, w[:, None, :].astype(x.dtype), window_strides=(1,), padding=[(k // 2, k // 2)],
        dimension_numbers=('NWC', 'WIO', 'NWC'), feature_group_count=x.shape[-1])

def ssd_chunked(xs, dt, a_coef, bm, cm):
    seq = xs.shape[0]
    nc = seq // SSD_CHUNK
    hpg = SSD_HEADS // SSD_GROUPS
    xdt = (xs * dt[..., None]).reshape(nc, SSD_CHUNK, SSD_GROUPS, hpg, SSD_HEAD_DIM)
    a = (dt * a_coef).astype(jnp.float32).reshape(nc, SSD_CHUNK, SSD_GROUPS, hpg)
    a_cs = jnp.cumsum(a, axis=1)
    bc = bm.reshape(nc, SSD_CHUNK, SSD_GROUPS, SSD_STATE)
    cc = cm.reshape(nc, SSD_CHUNK, SSD_GROUPS, SSD_STATE)
    lower = jnp.tril(jnp.ones((SSD_CHUNK, SSD_CHUNK), dtype=bool))
    seg = a_cs[:, :, None] - a_cs[:, None, :]
    decay = jnp.exp(jnp.where(lower[None, :, :, None, None], seg, -jnp.inf))
    cb = jnp.einsum('clgn,csgn->clsg', cc, bc)
    y_diag = jnp.einsum('clsg,clsgk,csgkp->clgkp', cb, decay, xdt)
    decay_to_end = jnp.exp(a_cs[:, -1:] - a_cs)
    states = jnp.einsum('csgn,csgk,csgkp->cgkpn', bc, decay_to_end, xdt)
    chunk_decay = jnp.exp(a_cs[:, -1])

    def step(carry, inp):
        st, dec = inp
        return carry * dec[..., None, None] + st, carry

    init = jnp.zeros(states.shape[1:], states.dtype)
    _, prev = lax.scan(step, init, (states, chunk_decay))
    y_off = jnp.einsum('clgn,cgkpn,clgk->clgkp', cc, prev, jnp.exp(a_cs))
    return (y_diag + y_off).reshape(seq, SSD_HEADS, SSD_HEAD_DIM).astype(xs.dtype)

def run_ssd(xs, dt, a_coef, bm, cm):
    return lax.map(lambda t: ssd_chunked(t[0], t[1], a_coef, t[2], t[3]), (xs, dt, bm, cm))

def ssd_mixer(x, w_in, conv_w, conv_b, dt_bias, a_log, d_skip, norm_w, w_out):
    bsz, seq, _ = x.shape
    zxbcdt = x @ w_in
    z = zxbcdt[..., :SSD_D_INNER]
    xbc = zxbcdt[..., SSD_D_INNER:SSD_D_INNER + SSD_CONV_DIM]
    dt_raw = zxbcdt[..., SSD_D_INNER + SSD_CONV_DIM:]
    xbc = jax.nn.silu(depthwise_conv(xbc, conv_w) + conv_b)
    gn = SSD_GROUPS * SSD_STATE
    xs = xbc[..., :SSD_D_INNER].reshape(bsz, seq, SSD_HEADS, SSD_HEAD_DIM)
    bm = xbc[..., SSD_D_INNER:SSD_D_INNER + gn].reshape(bsz, seq, SSD_GROUPS, SSD_STATE)
    cm = xbc[..., SSD_D_INNER + gn:].reshape(bsz, seq, SSD_GROUPS, SSD_STATE)
    dt = jax.nn.softplus(dt_raw.reshape(bsz, seq, 2, SSD_HEADS) + dt_bias)
    a_coef = -jnp.exp(a_log)
    y_fwd = run_ssd(xs, dt[:, :, 0], a_coef[0], bm, cm)
    flip = lambda t: jnp.flip(t, axis=1)
    y_bwd = flip(run_ssd(flip(xs), flip(dt[:, :, 1]), a_coef[1], flip(bm), flip(cm)))
    y = y_fwd + y_bwd + d_skip[:, None] * xs
    y = y.reshape(bsz, seq, SSD_D_INNER) * jax.nn.silu(z)
    return grouped_rmsnorm(y, norm_w) @ w_out

def short_conv_mixer(x, w_in, conv_w, w_out):
    d = x.shape[-1]
    bch = x @ w_in
    b_gate, c_gate, h = bch[..., :d], bch[..., d:2 * d], bch[..., 2 * d:]
    return (b_gate * depthwise_conv(c_gate * h, conv_w)) @ w_out

def na_mixer(x, w_qkv, rpb, w_out):
    bsz, seq, d = x.shape
    rows = seq // GRID_W
    wr = min(NA_WIN_ROWS, rows)
    nqb = GRID_W // NA_QCOL_BLOCK
    qkv = (x @ w_qkv).reshape(bsz, rows, GRID_W, 3, NA_HEADS, NA_HEAD_DIM)
    q = qkv[:, :, :, 0] * (NA_HEAD_DIM ** -0.5)
    k = qkv[:, :, :, 1]
    v = qkv[:, :, :, 2]
    r = jnp.arange(rows)
    key_rows = jnp.clip(r - wr // 2, 0, rows - wr)[:, None] + jnp.arange(wr)
    qcol = (jnp.arange(nqb) * NA_QCOL_BLOCK)[:, None] + jnp.arange(NA_QCOL_BLOCK)
    key_cols = (jnp.clip(qcol[:, 0] - NA_WIN_COLS // 2, 0, GRID_W - NA_KEY_COLS)[:, None]
                + jnp.arange(NA_KEY_COLS))
    col_start = jnp.clip(qcol - NA_WIN_COLS // 2, 0, GRID_W - NA_WIN_COLS)
    in_win = ((key_cols[:, None, :] >= col_start[..., None])
              & (key_cols[:, None, :] < col_start[..., None] + NA_WIN_COLS))
    dr_idx = key_rows - r[:, None] + NA_WIN_ROWS - 1
    dc_idx = jnp.clip(key_cols[:, None, :] - qcol[:, :, None] + NA_WIN_COLS - 1,
                      0, 2 * NA_WIN_COLS - 2)
    bias = rpb[:, dr_idx[:, None, None, :, None], dc_idx[None, :, :, None, :]]
    bias = jnp.where(in_win[None, None, :, :, None, :], bias.astype(jnp.float32), -jnp.inf)

    def one(t):
        qs, ks, vs = t
        qb = qs.reshape(rows, nqb, NA_QCOL_BLOCK, NA_HEADS, NA_HEAD_DIM)
        kg = ks[key_rows[:, None, :, None], key_cols[None, :, None, :]]
        vg = vs[key_rows[:, None, :, None], key_cols[None, :, None, :]]
        s = jnp.einsum('rcqhd,rcikhd->hrcqik', qb, kg).astype(jnp.float32) + bias
        shp = s.shape
        p = jax.nn.softmax(s.reshape(shp[:4] + (shp[4] * shp[5],)), axis=-1).reshape(shp)
        o = jnp.einsum('hrcqik,rcikhd->rcqhd', p.astype(vs.dtype), vg)
        return o.reshape(rows * GRID_W, NA_HEADS * NA_HEAD_DIM)

    return lax.map(one, (q, k, v)) @ w_out

def sq_relu_mlp(x, w_in, w_out):
    return jnp.square(jax.nn.relu(x @ w_in)) @ w_out

def setup_inputs(seed: int = 0) -> dict:
    key = jax.random.key(seed)
    ks = jax.random.split(key, 24)
    f32 = jnp.float32
    beta = (8.0 * DEPTH) ** -0.25
    nrm = lambda k, shape, scale: jax.random.normal(k, shape, f32) * scale
    x = nrm(ks[0], (BATCH, SEQ, D_MODEL), 1.0)
    ln_mix_g = 1.0 + nrm(ks[1], (DEPTH, D_MODEL), 0.02)
    ln_mix_b = nrm(ks[2], (DEPTH, D_MODEL), 0.02)
    ln_ffn_g = 1.0 + nrm(ks[3], (DEPTH, D_MODEL), 0.02)
    ln_ffn_b = nrm(ks[4], (DEPTH, D_MODEL), 0.02)
    ffn_w_in = nrm(ks[5], (DEPTH, D_MODEL, FFN_DIM), D_MODEL ** -0.5)
    ffn_w_out = nrm(ks[6], (DEPTH, FFN_DIM, D_MODEL), beta * FFN_DIM ** -0.5)
    ssd_w_in = nrm(ks[7], (N_SSD, D_MODEL, SSD_IN_DIM), D_MODEL ** -0.5)
    ssd_conv_w = nrm(ks[8], (N_SSD, SSD_CONV, SSD_CONV_DIM), SSD_CONV ** -0.5)
    ssd_conv_b = nrm(ks[9], (N_SSD, SSD_CONV_DIM), 0.01)
    dt0 = jnp.exp(jax.random.uniform(ks[10], (N_SSD, 2, SSD_HEADS), f32,
                                     math.log(DT_MIN), math.log(DT_MAX)))
    ssd_dt_bias = dt0 + jnp.log(-jnp.expm1(-dt0))
    ssd_a_log = jnp.log(jax.random.uniform(ks[11], (N_SSD, 2, SSD_HEADS), f32, 1.0, 16.0))
    ssd_d = 1.0 + nrm(ks[12], (N_SSD, SSD_HEADS), 0.02)
    ssd_norm_w = 1.0 + nrm(ks[13], (N_SSD, SSD_D_INNER), 0.02)
    ssd_w_out = nrm(ks[14], (N_SSD, SSD_D_INNER, D_MODEL), beta * SSD_D_INNER ** -0.5)
    sc_w_in = nrm(ks[15], (N_SC, D_MODEL, 3 * D_MODEL), D_MODEL ** -0.5)
    sc_conv_w = nrm(ks[16], (N_SC, SC_CONV, D_MODEL), SC_CONV ** -0.5)
    sc_w_out = nrm(ks[17], (N_SC, D_MODEL, D_MODEL), beta * D_MODEL ** -0.5)
    na_w_qkv = nrm(ks[18], (N_NA, D_MODEL, 3 * D_MODEL), D_MODEL ** -0.5)
    na_rpb = nrm(ks[19], (N_NA, NA_HEADS, 2 * NA_WIN_ROWS - 1, 2 * NA_WIN_COLS - 1), 0.02)
    na_w_out = nrm(ks[20], (N_NA, D_MODEL, D_MODEL), beta * D_MODEL ** -0.5)
    return {'x': x, 'ln_mix_g': ln_mix_g, 'ln_mix_b': ln_mix_b, 'ln_ffn_g': ln_ffn_g,
            'ln_ffn_b': ln_ffn_b, 'ffn_w_in': ffn_w_in, 'ffn_w_out': ffn_w_out,
            'ssd_w_in': ssd_w_in, 'ssd_conv_w': ssd_conv_w, 'ssd_conv_b': ssd_conv_b,
            'ssd_dt_bias': ssd_dt_bias, 'ssd_a_log': ssd_a_log, 'ssd_d': ssd_d,
            'ssd_norm_w': ssd_norm_w, 'ssd_w_out': ssd_w_out,
            'sc_w_in': sc_w_in, 'sc_conv_w': sc_conv_w, 'sc_w_out': sc_w_out,
            'na_w_qkv': na_w_qkv, 'na_rpb': na_rpb, 'na_w_out': na_w_out}

def reference(x, ln_mix_g, ln_mix_b, ln_ffn_g, ln_ffn_b, ffn_w_in, ffn_w_out,
              ssd_w_in, ssd_conv_w, ssd_conv_b, ssd_dt_bias, ssd_a_log, ssd_d,
              ssd_norm_w, ssd_w_out, sc_w_in, sc_conv_w, sc_w_out,
              na_w_qkv, na_rpb, na_w_out):
    alpha = (2.0 * DEPTH) ** 0.25
    for i in range(DEPTH):
        kind = i % N_MIXERS
        j = i // N_MIXERS
        if kind == 0:
            h = ssd_mixer(x, ssd_w_in[j], ssd_conv_w[j], ssd_conv_b[j], ssd_dt_bias[j],
                          ssd_a_log[j], ssd_d[j], ssd_norm_w[j], ssd_w_out[j])
        elif kind == 1:
            h = short_conv_mixer(x, sc_w_in[j], sc_conv_w[j], sc_w_out[j])
        else:
            h = na_mixer(x, na_w_qkv[j], na_rpb[j], na_w_out[j])
        x = layer_norm(alpha * x + h, ln_mix_g[i], ln_mix_b[i])
        x = layer_norm(alpha * x + sq_relu_mlp(x, ffn_w_in[i], ffn_w_out[i]),
                       ln_ffn_g[i], ln_ffn_b[i])
    return x


_drawn_inputs = setup_inputs


def setup_inputs(seed=0):
    import zlib

    import numpy as np

    out = dict(_drawn_inputs(seed))
    spreads = {}
    factors = {'ssd_conv_b': 8.0, 'ssd_d': 8.0, 'ssd_norm_w': 7.947, 'na_rpb': 43.934}
    for name, (base, spread) in spreads.items():
        noise = np.random.default_rng([zlib.crc32(name.encode()), seed]).standard_normal(out[name].shape)
        drawn = base * np.exp(spread * noise) if base else spread * noise
        out[name] = __import__('jax').numpy.asarray(drawn.astype(out[name].dtype))
    for name, factor in factors.items():
        out[name] = (out[name] * factor).astype(out[name].dtype)
    return out
```

```python
from contextlib import ExitStack

import concourse.bass as bass
from concourse import mybir

F32 = mybir.dt.float32
F32R = mybir.dt.float32r
ALU = mybir.AluOpType
ACT = mybir.ActivationFunctionType
AX = mybir.AxisListType

P = 128
D = 1024
SEQ = 256
NT = SEQ // P
KT = D // P
DEPTH = 4
ALPHA = (2.0 * DEPTH) ** 0.25
EPS = 1e-5
FFN = 4 * D

DI = 2 * D
HD = 64
HEADS = DI // HD
G = 8
NST = 128
HPG = HEADS // G
TAPS = 5
CONV_DIM = DI + 2 * G * NST
CT = CONV_DIM // P
GW = DI // G

SC_TAPS = 3

GRID_W = 64
ROWS = SEQ // GRID_W
NAH = 16
NAD = D // NAH
WIN_R, WIN_C = 8, 16
RPB_R, RPB_C = 2 * WIN_R - 1, 2 * WIN_C - 1
BLOCK_HEADS = 4

UNIT = 2048
COLS = UNIT // KT
RAW = 3
SPLIT = 4
ACTS = 4
HEAD_UNITS = 2
MLP_LAG = 3
E_HEAD = 768
E_PART = [(0, 256), (256, 128), (384, 256), (640, 128)]
GONE = -3.0e38

LAYERS = [("ssd", 0), ("conv", 0), ("attn", 0), ("ssd", 1)]


def plan_units(layers):
    units, subs = [], []

    def add(names, kind, j, b):
        names[(kind, b)] = len(units)
        units.append((kind, j, b))

    for i, (kind, j) in enumerate(layers):
        names = {}
        if kind == "ssd":
            for g in range(G + 3):
                if g < G:
                    add(names, "z", j, g)
                    if g == 0:
                        add(names, "dt", j, 0)
                    add(names, "bc", j, g)
                if g >= 3:
                    add(names, "so", j, g - 3)
                if g < G:
                    add(names, "x", j, g)
        elif kind == "conv":
            for b in range(5):
                if b < 4:
                    for what in ("cc", "ch", "cb"):
                        add(names, what, j, b)
                if b >= 1:
                    add(names, "co", j, b - 1)
        else:
            for b in range(6):
                if b < 4:
                    for what in ("v", "q", "k"):
                        add(names, what, j, b)
                if b >= 2:
                    add(names, "no", j, b - 2)
        subs.append((kind, j, names))
        names = {}
        for b in range(FFN // COLS + MLP_LAG):
            if b < FFN // COLS:
                add(names, "fi", i, b)
            if b >= MLP_LAG:
                add(names, "fo", i, b - MLP_LAG)
        subs.append(("ffn", i, names))
    return units, subs


def build(nc, x, ln_mix_g, ln_mix_b, ln_ffn_g, ln_ffn_b, ffn_w_in, ffn_w_out, ssd_w_in, ssd_conv_w,
          ssd_conv_b, ssd_dt_bias, ssd_a_log, ssd_d, ssd_norm_w, ssd_w_out, sc_w_in, sc_conv_w,
          sc_w_out, na_w_qkv, na_rpb, na_w_out, out):
    units, subs = plan_units(LAYERS)
    n_ssd = ssd_w_in.shape[0]

    def weight_parts(u):
        kind, j, b = units[u]

        def cols(w, c0, n):
            return w[j].rearrange("(k p) n -> p k n", p=P)[:, :, c0:c0 + n]

        if kind == "dt":
            return [(cols(ssd_w_in, DI + CONV_DIM, 2 * HEADS), 0, 2 * HEADS)], KT, 2 * HEADS
        if kind == "bc":
            return [(cols(ssd_w_in, 2 * DI + b * NST, NST), 0, NST),
                    (cols(ssd_w_in, 2 * DI + (G + b) * NST, NST), NST, 2 * NST)], KT, COLS
        start = {"x": (ssd_w_in, DI), "z": (ssd_w_in, 0), "fi": (ffn_w_in, 0),
                 "cb": (sc_w_in, 0), "cc": (sc_w_in, D), "ch": (sc_w_in, 2 * D),
                 "q": (na_w_qkv, 0), "k": (na_w_qkv, D), "v": (na_w_qkv, 2 * D)}
        if kind in start:
            w, c0 = start[kind]
            return [(cols(w, c0 + b * COLS, COLS), 0, COLS)], KT, COLS
        w = {"so": ssd_w_out, "co": sc_w_out, "no": na_w_out, "fo": ffn_w_out}[kind]
        return [(w[j].rearrange("(k p) n -> p k n", p=P)[:, 2 * b:2 * b + 2, :], 0, D)], 2, D

    with ExitStack() as ctx:
        def sb(name, shape, dt=F32):
            return ctx.enter_context(nc.sbuf_tensor(name, shape, dt))

        def sem(name):
            return ctx.enter_context(nc.semaphore(name))

        raw = sb("raw", [P, RAW, UNIT])
        w_high = sb("w_high", [P, SPLIT, UNIT], F32R)
        w_low = sb("w_low", [P, SPLIT, UNIT], F32R)
        xT = sb("xT", [P, KT, 2, SEQ], F32R)
        opT = sb("opT", [P, ACTS, 2, 2, SEQ], F32R)
        xs = sb("x_tokens", [P, NT, D])
        gb = sb("ln_gain_bias", [P, 2, D])
        E = sb("E", [P, 2, HPG * E_HEAD])
        ssd_rows = E[0:CT, 0, 0:n_ssd * (TAPS + 2) * P].rearrange("c (j q p) -> c j q p", j=n_ssd, p=P)
        sc_rows = E[0:KT, 1, 0:SC_TAPS * P].rearrange("c (q p) -> c q p", p=P)
        tri_a = sb("ring_a", [P, 3, 512])
        tri_b = sb("ring_b", [P, 3, 512])
        tri_c = sb("ring_c", [P, 3, 512])
        pad = sb("conv_pad", [P, 2, 2, SEQ + TAPS - 1])
        conv = sb("conv", [P, 2, 2, SEQ])
        th = sb("tanh", [P, 2, 512])
        xsT = sb("xsT", [P, 2, 2, SEQ])
        gate = sb("gate", [P, 512])
        sq = sb("square", [P, 512])
        ident = sb("ident", [P, P])
        ones = sb("ones", [P, P])
        prefix = sb("prefix", [P, P])
        suffix = sb("suffix", [P, P])
        ssd_par = sb("ssd_par", [P, n_ssd, TAPS + 2, CT])
        sc_par = sb("sc_par", [P, SC_TAPS, KT])
        dt_bias = sb("dt_bias", [P, n_ssd, 2 * HEADS])
        a_neg = sb("a_neg", [P, n_ssd, 2 * HEADS])
        skip = sb("skip", [P, n_ssd, HEADS])
        dts = sb("dts", [P, NT, 2 * HEADS])
        dtt = xsT[:, :, :, :].rearrange("p a b c -> p (a b c)")[:, 0:6 * NT * 2 * HEADS].rearrange(
            "p (q t c) -> p q t c", q=6, t=NT)
        cs = sb("cumsum", [P, NT, 2 * HEADS])
        ncs = sb("neg_cumsum", [P, NT, 2 * HEADS])
        csT = sb("cumsum_rows", [2 * HEADS, SEQ])
        stats = sb("stats", [P, 2, 6])
        mv = sb("mean_var", [P, 2])
        small = sb("small", [P, 16])
        half_neg = sb("minus_half", [P, 2])
        att = sb("softmax_stats", [P, 2, 8])
        rows_dram = nc.dram_tensor("cumsum_dram", [n_ssd, 2 * HEADS, SEQ], F32, kind="Internal").ap()

        Y = [[ctx.enter_context(nc.psum_tensor(f"y{t}{n}", [P, 512], F32)) for n in range(2)] for t in range(NT)]
        A = [ctx.enter_context(nc.psum_tensor(f"acc{n}", [P, 512], F32)) for n in range(2)]
        I = [ctx.enter_context(nc.psum_tensor(f"inner{n}", [P, 512], F32)) for n in range(2)]

        raw_landed = [sem(f"raw_landed{n}") for n in range(RAW)]
        x_landed = sem("x_landed")
        par_landed = sem("par_landed")
        gb_landed = sem("gb_landed")
        rows_stored = sem("rows_stored")
        e_landed = [sem(f"e_landed{n}") for n in range(2)]
        bias_landed = [sem(f"bias_landed{n}") for n in range(4)]
        out_stored = sem("out_stored")
        w_high_done, w_low_done, w_used = sem("w_high_done"), sem("w_low_done"), sem("w_used")
        consts, par_turned, par_done, a_done = sem("consts"), sem("par_turned"), sem("par_done"), sem("a_done")
        y_ready, y_free = sem("y_ready"), sem("y_free")
        var_done, rstd_done = sem("var_done"), sem("rstd_done")
        ln_out, xt_turned = sem("ln_out"), sem("xt_turned")
        xt_high, xt_low = sem("xt_high"), sem("xt_low")
        op_turned, op_high, op_low = sem("op_turned"), sem("op_high"), sem("op_low")
        relu_done, square_done = sem("relu_done"), sem("square_done")
        dt_biased, dt_exp = sem("dt_biased"), sem("dt_exp")
        a_steps, cs_acc, cs_copied, ncs_done = sem("a_steps"), sem("cs_acc"), sem("cs_copied"), sem("ncs_done")
        cs_turned, cs_rows = sem("cs_turned"), sem("cs_rows")
        pad_filled, first_tap, taps_done = sem("pad_filled"), sem("first_tap"), sem("taps_done")
        tanh_done, silu_done = sem("tanh_done"), sem("silu_done")
        xs_turned, xs_copied = sem("xs_turned"), sem("xs_copied")
        e_masked, e_exp, cb_ready, g_done = sem("e_masked"), sem("e_exp"), sem("cb_ready"), sem("g_done")
        yg_ready, y_added, gated = sem("yg_ready"), sem("y_added"), sem("gated")
        msq_done, rms_done, scaled = sem("msq_done"), sem("rms_done"), sem("scaled")
        sc_c, sc_prod, sc_gated = sem("sc_c"), sem("sc_prod"), sem("sc_gated")
        qkv_done = sem("qkv_done")
        s_ready, s_biased, s_max, p_done = sem("s_ready"), sem("s_biased"), sem("s_max"), sem("p_done")
        pt_ready, pt_done, o_ready, o_done = sem("pt_ready"), sem("pt_done"), sem("o_ready"), sem("o_done")
        bias_masked, p_scale = sem("bias_masked"), sem("p_scale")
        act_step, dve_step, pool_step = sem("act_step"), sem("dve_step"), sem("pool_step")

        def f(ap):
            return ap.bitcast(F32)

        def views(base):
            return base.rearrange("p (a b) -> p a b", a=2)

        bias_b = [E[:, 0, n * 512:(n + 1) * 512] for n in range(4)]
        prob_b = [E[:, 0, (4 + n) * 512:(5 + n) * 512] for n in range(2)]
        probT_b = [E[:, 1, n * 512:(n + 1) * 512] for n in range(2)]
        o_b = [E[:, 1, (2 + n) * 512:(3 + n) * 512] for n in range(2)]

        n_par_dmas = n_ssd * 6 + 1
        out_units = [u for u, (kind, _, _) in enumerate(units) if kind in ("so", "co", "no", "fo")]
        in_units = [u for u in range(len(units)) if u not in out_units]
        acc_of = {u: A[k % 2] for k, u in enumerate(in_units)}
        inner_of = {}
        last_unit = [max(names.values()) for _, _, names in subs]

        block = ctx.enter_context(nc.Block())

        @block.sync
        def _(sp):
            for t in range(NT):
                sp.dma_start(xs[:, t, :], x[0, t * P:(t + 1) * P, :]).then_inc(x_landed, 16)
            for u in range(len(units)):
                parts, k, n = weight_parts(u)
                if u >= RAW:
                    sp.wait_ge(w_high_done, u - RAW + 1)
                    sp.wait_ge(w_low_done, u - RAW + 1)
                dst = raw[:, u % RAW, 0:k * n].rearrange("p (k n) -> p k n", k=k)
                if len(parts) == 1:
                    src = parts[0][0]
                    sp.dma_start(dst[:, 0:k // 2, :], src[:, 0:k // 2, :]).then_inc(raw_landed[u % RAW], 16)
                    sp.dma_start(dst[:, k // 2:k, :], src[:, k // 2:k, :]).then_inc(raw_landed[u % RAW], 16)
                else:
                    for src, c0, c1 in parts:
                        sp.dma_start(dst[:, :, c0:c1], src).then_inc(raw_landed[u % RAW], 16)
            last = len(subs) - 1
            for t in range(NT):
                sp.wait_ge(ln_out, 4 * last + 2 * t + 2)
                sp.dma_start(out[0, t * P:(t + 1) * P, :], xs[:, t, :]).then_inc(out_stored, 16)
            sp.wait_ge(out_stored, 16 * NT)

        @block.gpsimd
        def _(pool):
            step = [0]

            def own(ins):
                ins.then_inc(pool_step, 1)
                step[0] += 1
                pool.wait_ge(pool_step, step[0])

            for j in range(n_ssd):
                pool.dma_start(ssd_rows[:, j, 0:TAPS, :],
                               ssd_conv_w[j].rearrange("a (c p) -> c a p", p=P)).then_inc(par_landed, 16)
                pool.dma_start(ssd_rows[:, j, TAPS, :],
                               ssd_conv_b[j].rearrange("(c p) -> c p", p=P)).then_inc(par_landed, 16)
                pool.dma_start(ssd_rows[0:DI // P, j, TAPS + 1, :],
                               ssd_norm_w[j].rearrange("(c p) -> c p", p=P)).then_inc(par_landed, 16)
                pool.dma_start(dt_bias[:, j, :], ssd_dt_bias[j:j + 1].rearrange("a b c -> a (b c)")
                               .to_broadcast([P, 2 * HEADS])).then_inc(par_landed, 16)
                pool.dma_start(a_neg[:, j, :], ssd_a_log[j:j + 1].rearrange("a b c -> a (b c)")
                               .to_broadcast([P, 2 * HEADS])).then_inc(par_landed, 16)
                pool.dma_start(skip[:, j, :], ssd_d[j:j + 1].to_broadcast([P, HEADS])).then_inc(par_landed, 16)
            pool.dma_start(sc_rows[:, :, :], sc_conv_w[0].rearrange("a (c p) -> c a p", p=P)).then_inc(par_landed, 16)
            own(nc.gpsimd.memset(ident[:, :], 0.0))
            own(nc.gpsimd.affine_select(out=ident[:, :], in_=ident[:, :], compare_op=ALU.not_equal, fill=1.0,
                                        base=0, pattern=[[-1, P]], channel_multiplier=1))
            own(nc.gpsimd.memset(ones[:, :], 1.0))
            own(nc.gpsimd.affine_select(out=prefix[:, :], in_=ones[:, :], compare_op=ALU.is_ge, fill=0.0,
                                        base=0, pattern=[[1, P]], channel_multiplier=-1))
            own(nc.gpsimd.affine_select(out=suffix[:, :], in_=ones[:, :], compare_op=ALU.is_ge, fill=0.0,
                                        base=0, pattern=[[-1, P]], channel_multiplier=1))
            own(nc.gpsimd.memset(pad[:, :, :, :], 0.0))
            nc.gpsimd.memset(half_neg[:, :], -0.5).then_inc(consts, 1)
            pool.wait_ge(consts, 1)
            group = [0]
            head = [0]

            def load_gain_bias(s):
                g_src, b_src = (ln_ffn_g, ln_ffn_b) if s % 2 else (ln_mix_g, ln_mix_b)
                if s:
                    pool.wait_ge(ln_out, 4 * s)
                pool.dma_start(gb[:, 0, :], g_src[s // 2:s // 2 + 1, :].to_broadcast([P, D])).then_inc(gb_landed, 16)
                pool.dma_start(gb[:, 1, :], b_src[s // 2:s // 2 + 1, :].to_broadcast([P, D])).then_inc(gb_landed, 16)

            def ln_power(s):
                for t in range(NT):
                    pool.wait_ge(var_done, 2 * s + t + 1)
                    nc.gpsimd.tensor_tensor(small[:, 2 + t:3 + t], small[:, t:t + 1], half_neg[:, 0:1],
                                            ALU.pow).then_inc(rstd_done, 1)

            for s, (kind, j, names) in enumerate(subs):
                load_gain_bias(s)
                if kind == "ssd":
                    first = group[0]
                    rows = rows_dram[j]
                    pool.wait_ge(rows_stored, 16 * (first // G + 1))
                    for g in range(G + 1):
                        if g < G:
                            n = first + g
                            if n >= 2:
                                pool.wait_ge(yg_ready, n - 1)
                            slot = E[:, n % 2, :].rearrange("p (h e) -> p h e", h=HPG)
                            for q, (off, width) in enumerate(E_PART):
                                back = q in (1, 2)
                                l0 = P if q == 3 else 0
                                r0 = (HEADS if back else 0) + g * HPG
                                src = rows[r0:r0 + HPG, l0:l0 + width]
                                src = bass.AP(src.tensor, src.offset, [[0, P], [SEQ, HPG], [1, width]])
                                pool.dma_start(slot[:, :, off:off + width], src).then_inc(e_landed[n % 2], 16)
                            pool.wait_ge(e_landed[n % 2], 64 * (n // 2 + 1))
                            for q, (off, sign) in enumerate(((0, 1), (256, -1), (384 + P, -1), (640, 1))):
                                v = slot[:, :, off:off + P]
                                ins = nc.gpsimd.affine_select(out=v, in_=v, compare_op=ALU.is_ge, fill=GONE, base=0,
                                                              pattern=[[0, HPG], [sign, P]], channel_multiplier=-sign)
                            ins.then_inc(e_masked, 1)
                        if g >= 1:
                            n = first + g - 1
                            pool.wait_ge(msq_done, n + 1)
                            own(nc.gpsimd.tensor_scalar(small[:, 6:8], small[:, 4:6], 1.0 / GW, EPS, ALU.mult, ALU.add))
                            nc.gpsimd.tensor_tensor(small[:, 8:10], small[:, 6:8], half_neg[:, :], ALU.pow).then_inc(rms_done, 1)
                    group[0] += G
                if kind == "attn":
                    def mask_bias(h):
                        pool.wait_ge(bias_landed[h % 4], 16 * ROWS * (h // 4 + 1))
                        edge = GRID_W - WIN_C
                        for half in range(2):
                            v = bias_b[h % 4][64 * half:64 * half + 64, :].rearrange("p (a c) -> p a c", c=GRID_W)
                            own(nc.gpsimd.affine_select(out=v[:, :, 0:edge], in_=v[:, :, 0:edge], compare_op=ALU.is_ge,
                                                        fill=GONE, base=WIN_C // 2 - GRID_W + 1,
                                                        pattern=[[0, 2 * ROWS], [1, edge]], channel_multiplier=1))
                            ins = nc.gpsimd.affine_select(out=v[:, :, WIN_C:], in_=v[:, :, WIN_C:], compare_op=ALU.is_ge,
                                                          fill=GONE, base=GRID_W - 1 + WIN_C // 2 - 1 - WIN_C,
                                                          pattern=[[0, 2 * ROWS], [-1, edge]], channel_multiplier=-1)
                        ins.then_inc(bias_masked, 1)

                    for h in range(NAH):
                        if h >= 4:
                            pool.wait_ge(s_biased, h - 3)
                        if h == 0:
                            pool.wait_ge(par_turned, n_ssd + 1)
                            if s:
                                pool.wait_ge(ln_out, 4 * s)
                        for r in range(ROWS):
                            src = bass.AP(na_rpb.tensor, na_rpb.offset + (h * RPB_R + WIN_R - 1 - r) * RPB_C
                                          + WIN_C - GRID_W, [[1, GRID_W], [RPB_C, ROWS], [1, GRID_W]])
                            c0 = (r // 2) * SEQ
                            dst = bias_b[h % 4][64 * (r % 2):64 * (r % 2) + 64, c0:c0 + SEQ]
                            pool.dma_start(dst.rearrange("p (a b) -> p a b", a=ROWS), src).then_inc(bias_landed[h % 4], 16)
                        if h >= 1:
                            mask_bias(h - 1)
                    mask_bias(NAH - 1)
                ln_power(s)

        @block.tensor
        def _(pe):
            acc_freed = []
            inn_freed = []
            n = dict.fromkeys(["conv", "z", "mlp", "op", "grp", "silu", "sc", "qkv", "head", "dt", "opu"], 0)

            def acc_bank(freed_by):
                k = len(acc_freed)
                if k >= 2:
                    pe.wait_ge(*acc_freed[k - 2])
                acc_freed.append(freed_by)
                return A[k % 2]

            def inner_bank(key, freed_by):
                k = len(inn_freed)
                inner_of[key] = I[k % 2]
                if k >= 2:
                    pe.wait_ge(*inn_freed[k - 2])
                inn_freed.append(freed_by)
                return I[k % 2]

            def weights(u):
                pe.wait_ge(w_high_done, u + 1)
                pe.wait_ge(w_low_done, u + 1)
                return w_high[:, u % SPLIT, :], w_low[:, u % SPLIT, :]

            def features(u, bank, ts):
                wh, wl = weights(u)
                span = slice(ts[0] * P, (ts[-1] + 1) * P)
                for c in range(2):
                    for k in range(KT):
                        col = k * COLS + c * P
                        for part, (w, low) in enumerate(((wh, 0), (wh, 1), (wl, 0))):
                            mm = nc.tensor.matmul(bank[:, c * SEQ:(c + 1) * SEQ][:, span], w[:, col:col + P],
                                                  xT[:, k, low, span], start=(k == 0 and part == 0),
                                                  stop=(k == KT - 1 and part == 2))
                return mm

            def tokens(u, bank, ts, width):
                wh, wl = weights(u)
                for t in ts:
                    for k in range(KT):
                        for part, (w, low) in enumerate(((wh, 0), (wh, 1), (wl, 0))):
                            mm = nc.tensor.matmul(bank[:, t * width:(t + 1) * width], xT[:, k, low, t * P:(t + 1) * P],
                                                  w[:, k * width:(k + 1) * width], start=(k == 0 and part == 0),
                                                  stop=(k == KT - 1 and part == 2))
                return mm

            def used(mm):
                mm.then_inc(w_used, 1)

            FORM = {"bc": features, "x": features, "z": tokens, "dt": tokens, "fi": features, "cb": features,
                    "cc": features, "ch": features, "q": features, "k": features, "v": tokens}

            def freed_by(kind):
                if kind in ("bc", "x"):
                    n["conv"] += 1
                    return pad_filled, n["conv"]
                if kind == "z":
                    n["z"] += 1
                    return silu_done, 3 * n["z"] - 2
                if kind == "dt":
                    n["dt"] += 1
                    return dt_biased, n["dt"]
                if kind == "fi":
                    n["mlp"] += 1
                    return relu_done, n["mlp"]
                if kind in ("q", "k", "v"):
                    n["qkv"] += 1
                    return qkv_done, n["qkv"]
                n["sc"] += 1
                c = (n["sc"] - 1) // 3 + 1
                return {"cc": sc_c, "ch": sc_prod, "cb": sc_gated}[kind], c

            def project(u, ts, bank=None):
                kind = units[u][0]
                if bank is None:
                    bank = acc_bank(freed_by(kind))
                form = tokens if kind == "fi" and units[u][2] < HEAD_UNITS else FORM[kind]
                if form is features:
                    mm = features(u, bank, ts)
                else:
                    mm = tokens(u, bank, ts, 2 * HEADS if kind == "dt" else COLS)
                if ts[-1] == NT - 1:
                    used(mm)
                return bank

            def turn_x(s, t):
                for half in range(2):
                    if s:
                        pe.wait_ge(ln_out, 4 * (s - 1) + 2 * t + half + 1)
                    else:
                        pe.wait_ge(x_landed, 16 * NT)
                    bank = inner_bank(("xt", s, t, half), (xt_low, 4 * s + 2 * t + half + 1))
                    for q in range(4):
                        c = (4 * half + q) * P
                        mm = nc.tensor.transpose(bank[:, q * P:(q + 1) * P], xs[:, t, c:c + P], ident[:, :])
                    mm.then_inc(xt_turned, 1)

            def head_units(s, us):
                banks = {}
                for t in range(NT):
                    turn_x(s, t)
                    pe.wait_ge(xt_high, 4 * s + 2 * t + 2)
                    pe.wait_ge(xt_low, 4 * s + 2 * t + 2)
                    for u in us:
                        banks[u] = project(u, [t], banks.get(u))

            def out_part(s, u, o, first, last, ts):
                wh, wl = weights(u)
                pe.wait_ge(op_high, o + 1)
                pe.wait_ge(op_low, o + 1)
                for t in ts:
                    if first and s:
                        pe.wait_ge(y_free, 2 * (s - 1) + t + 1)
                    for k in range(2):
                        for low, w in ((0, wh), (0, wl), (1, wh)):
                            for c in range(2):
                                mm = nc.tensor.matmul(Y[t][c][:, :], opT[:, o % ACTS, low, k, t * P:(t + 1) * P],
                                                      w[:, k * D + c * 512:k * D + (c + 1) * 512],
                                                      start=(first and k == 0 and low == 0 and w is wh),
                                                      stop=(last and k == 1 and low == 1))
                return mm

            def out_unit(s, u, first=False):
                o = n["opu"]
                n["opu"] += 1
                out_part(s, u, o, first, False, range(NT)).then_inc(w_used, 1)

            def tail(s, us, first=False):
                o = n["opu"]
                n["opu"] += len(us)
                for t in range(NT):
                    for i, u in enumerate(us):
                        mm = out_part(s, u, o + i, first and i == 0, i == len(us) - 1, [t])
                        if t == NT - 1:
                            mm.then_inc(w_used, 1)
                    if t == 0:
                        mm.then_inc(y_ready, 1)

            pe.wait_ge(par_landed, 16 * n_par_dmas)
            pe.wait_ge(consts, 1)
            for j in range(n_ssd):
                bank = inner_bank(("par", j), (par_done, 2 * (j + 1)))
                for q in range(TAPS + 2):
                    rows = CT if q <= TAPS else DI // P
                    mm = nc.tensor.transpose(bank[:, q * CT:q * CT + rows], ssd_rows[0:rows, j, q, :], ident[0:rows, 0:rows])
                mm.then_inc(par_turned, 1)
            bank = inner_bank(("par", n_ssd), (par_done, 2 * n_ssd + 1))
            for q in range(SC_TAPS):
                mm = nc.tensor.transpose(bank[:, q * KT:(q + 1) * KT], sc_rows[:, q, :], ident[0:KT, 0:KT])
            mm.then_inc(par_turned, 1)

            for s, (kind, j, names) in enumerate(subs):
                if kind == "ffn":
                    last = FFN // COLS - 1
                    head_units(s, [names[("fi", b)] for b in range(HEAD_UNITS)])
                    for b in range(HEAD_UNITS, last + 1):
                        project(names[("fi", b)], range(NT))
                        if b < 2 * HEAD_UNITS:
                            o = n["op"] + b - HEAD_UNITS
                            pe.wait_ge(square_done, 16 * (s // 2) + b - HEAD_UNITS + 1)
                            bank = inner_bank(("op", o), (op_low, o + 1))
                            for c in range(2):
                                for t in range(NT):
                                    mm = nc.tensor.transpose(bank[:, c * SEQ + t * P:c * SEQ + (t + 1) * P],
                                                             conv[:, o % 2, t, c * P:(c + 1) * P], ident[:, :])
                            mm.then_inc(op_turned, 1)
                        if b >= MLP_LAG:
                            out_unit(s, names[("fo", b - MLP_LAG)], first=(b == MLP_LAG))
                    tail(s, [names[("fo", last + 1 - q)] for q in range(MLP_LAG, 0, -1)])
                elif kind == "ssd":
                    n0 = n["grp"]
                    n["grp"] += G
                    head_units(s, [names[("z", 0)], names[("dt", 0)]])

                    def cumsum():
                        pe.wait_ge(a_steps, n0 // G + 1)
                        bank = inner_bank(("cs", j), (ncs_done, n0 // G + 1))
                        a = dtt[:, 5, :, :]
                        H = HEADS
                        for t, c, terms in ((0, 0, ((prefix, 0),)), (0, H, ((suffix, 0), (ones, 1))),
                                            (1, 0, ((ones, 0), (prefix, 1))), (1, H, ((suffix, 1),))):
                            for i, (m, src) in enumerate(terms):
                                mm = nc.tensor.matmul(bank[:, t * 2 * H + c:t * 2 * H + c + H], m[:, :], a[:, src, c:c + H],
                                                      start=(i == 0), stop=(i == len(terms) - 1))
                        mm.then_inc(cs_acc, 1)

                    def cumsum_rows():
                        pe.wait_ge(cs_copied, n0 // G + 1)
                        bank = inner_bank(("cs_rows", j), (cs_rows, n0 // G + 1))
                        for t in range(NT):
                            mm = nc.tensor.transpose(bank[0:2 * HEADS, t * P:(t + 1) * P], cs[:, t, :], ident[:, :])
                        mm.then_inc(cs_turned, 1)

                    for i in range(G + 3):
                        g, k = i, n0 + i
                        if 0 < i < G:
                            project(names[("z", g)], range(NT))
                        if 1 <= i <= G:
                            m = k - 1
                            pe.wait_ge(silu_done, 3 * (m + 1))
                            bank = inner_bank(("xs", m), (xs_copied, m + 1))
                            for t in range(NT):
                                for c in range(2):
                                    mm = nc.tensor.transpose(bank[:, t * GW + c * P:t * GW + (c + 1) * P],
                                                             xsT[:, m % 2, c, t * P:(t + 1) * P], ident[:, :])
                            mm.then_inc(xs_turned, 1)
                        if i >= 3:
                            m = k - 3
                            o = n["op"]
                            n["op"] += 1
                            pe.wait_ge(scaled, m + 1)
                            bank = inner_bank(("op", o), (op_low, o + 1))
                            for c in range(2):
                                for t in range(NT):
                                    mm = nc.tensor.transpose(bank[:, c * SEQ + t * P:c * SEQ + (t + 1) * P],
                                                             gate[:, t * GW + c * P:t * GW + (c + 1) * P], ident[:, :])
                            mm.then_inc(op_turned, 1)
                        if 2 <= i < G + 2:
                            m = k - 2
                            pe.wait_ge(silu_done, 3 * m + 2)
                            bank = inner_bank(("cb", m), (g_done, m + 1))
                            bc = tri_a[:, m % 3, :]
                            for t in range(NT):
                                mm = nc.tensor.matmul(bank[:, t * SEQ:(t + 1) * SEQ], bc[:, t * P:(t + 1) * P],
                                                      bc[:, SEQ:2 * SEQ], start=True, stop=True)
                            mm.then_inc(cb_ready, 1)
                        if i < G:
                            project(names[("bc", g)], range(NT))
                        if i == 0:
                            cumsum()
                        if i >= 3 and i < G + 2:
                            out_unit(s, names[("so", i - 3)], first=(i == 3))
                        if i < G:
                            project(names[("x", g)], range(NT))
                        if i == 0:
                            cumsum_rows()
                        if 2 <= i < G + 2:
                            m = k - 2
                            pe.wait_ge(g_done, m + 1)
                            pe.wait_ge(xs_copied, m + 1)
                            bank = inner_bank(("yg", m), (y_added, m + 1))
                            for h in range(HPG):
                                e = E[:, m % 2, h * E_HEAD:(h + 1) * E_HEAD]
                                x0 = tri_b[:, m % 3, h * HD:(h + 1) * HD]
                                x1 = tri_b[:, m % 3, GW + h * HD:GW + (h + 1) * HD]
                                for t, terms in ((0, ((0, x0), (256, x0), (384, x1))),
                                                 (1, ((P, x0), (640, x1), (384 + P, x1)))):
                                    for q, (c, v) in enumerate(terms):
                                        mm = nc.tensor.matmul(bank[:, t * GW + h * HD:t * GW + (h + 1) * HD],
                                                              e[:, c:c + P], v, start=(q == 0), stop=(q == 2))
                            mm.then_inc(yg_ready, 1)
                    tail(s, [names[("so", G - 1)]])
                elif kind == "conv":
                    head_units(s, [])
                    for b in range(5):
                        if b < 4:
                            project(names[("cc", b)], range(NT))
                            project(names[("ch", b)], range(NT))
                            project(names[("cb", b)], range(NT))
                        if 1 <= b < 3:
                            out_unit(s, names[("co", b - 1)], first=(b == 1))
                    tail(s, [names[("co", 2)], names[("co", 3)]])
                else:
                    head_units(s, [names[("v", 0)]])

                    def scores(h):
                        blk, hh = h // BLOCK_HEADS, h % BLOCK_HEADS
                        pe.wait_ge(qkv_done, 3 * blk + 3)
                        bank = inner_bank(("s", h), (s_biased, h + 1))
                        rows, c = slice(64 * (hh % 2), 64 * (hh % 2) + 64), (hh // 2) * SEQ
                        for t in range(NT):
                            mm = nc.tensor.matmul(bank[:, t * SEQ:(t + 1) * SEQ],
                                                  tri_a[rows, blk % 3, c + t * P:c + (t + 1) * P],
                                                  tri_b[rows, blk % 3, c:c + SEQ], start=True, stop=True)
                        mm.then_inc(s_ready, 1)

                    def turn_probs(h):
                        pe.wait_ge(p_done, h + 1)
                        bank = inner_bank(("pt", h), (pt_done, h + 1))
                        for k in range(NT):
                            for t in range(NT):
                                mm = nc.tensor.transpose(bank[:, k * SEQ + t * P:k * SEQ + (t + 1) * P],
                                                         prob_b[h % 2][:, t * SEQ + k * P:t * SEQ + (k + 1) * P], ident[:, :])
                        mm.then_inc(pt_ready, 1)

                    def mix_values(h):
                        blk, hh = h // BLOCK_HEADS, h % BLOCK_HEADS
                        pe.wait_ge(pt_done, h + 1)
                        bank = inner_bank(("o", h), (o_done, h + 1))
                        for t in range(NT):
                            for k in range(NT):
                                mm = nc.tensor.matmul(bank[:, t * NAD:(t + 1) * NAD],
                                                      probT_b[h % 2][:, k * SEQ + t * P:k * SEQ + (t + 1) * P],
                                                      tri_c[:, blk % 3, k * COLS + hh * NAD:k * COLS + (hh + 1) * NAD],
                                                      start=(k == 0), stop=(k == NT - 1))
                        mm.then_inc(o_ready, 1)

                    def turn_out(blk):
                        o = n["op"]
                        n["op"] += 1
                        pe.wait_ge(o_done, BLOCK_HEADS * (blk + 1))
                        bank = inner_bank(("op", o), (op_low, o + 1))
                        for c in range(2):
                            for t in range(NT):
                                mm = nc.tensor.transpose(bank[:, c * SEQ + t * P:c * SEQ + (t + 1) * P],
                                                         o_b[blk % 2][:, t * COLS + c * P:t * COLS + (c + 1) * P], ident[:, :])
                        mm.then_inc(op_turned, 1)

                    for b in range(6):
                        for k in range(4):
                            h = 4 * (b - 1) + k
                            if 0 <= h < NAH:
                                scores(h)
                            if k < 3 and b < 4 and (b or k):
                                project(names[("vqk"[k], b)], range(NT))
                            if k == 3 and 2 <= b < 4:
                                out_unit(s, names[("no", b - 2)], first=(b == 2))
                            if 1 <= h <= NAH:
                                mix_values(h - 1)
                            if 0 <= h < NAH:
                                turn_probs(h)
                            if k == 1 and b >= 2:
                                turn_out(b - 2)
                    tail(s, [names[("no", 2)], names[("no", 3)]])
                if kind in ("ffn", "conv"):
                    n["op"] += FFN // COLS if kind == "ffn" else 4

        def spread(ap, dims):
            return bass.AP(ap.tensor, ap.offset, [list(ap.ap[0])] + dims)

        def reversed_rows(bank):
            ap = bank[:, :]
            return bass.AP(ap.tensor, ap.offset + GRID_W - 1, [list(ap.ap[0]), [GRID_W, 2 * ROWS], [-1, GRID_W]])

        def grid_rows(ap):
            return ap.rearrange("p a b -> p (a b)").rearrange("p (a c) -> p a c", c=GRID_W)

        def tap(j, q, ct):
            return ssd_par[:, j, q, ct:ct + 1]

        def channel_tiles(kind, g):
            return (2 * g, 2 * g + 1) if kind == "x" else (2 * G + g, 3 * G + g)

        @block.scalar
        def _(act):
            n = dict.fromkeys(["split", "step", "op", "turned", "grp", "conv", "th", "mlp"], 0)

            def split_to(last):
                while n["split"] <= min(last, len(units) - 1):
                    u = n["split"]
                    n["split"] += 1
                    _, k, c = weight_parts(u)
                    act.wait_ge(raw_landed[u % RAW], 32 * (u // RAW + 1))
                    if u >= SPLIT:
                        act.wait_ge(w_used, u - SPLIT + 1)
                    nc.scalar.activation(w_high[:, u % SPLIT, 0:k * c], raw[:, u % RAW, 0:k * c],
                                         ACT.Copy).then_inc(w_high_done, 1)

            def result(u):
                split_to(u + 3)
                act.wait_ge(w_used, u + 1)
                return acc_of[u]

            def operand(o):
                if o >= ACTS:
                    act.wait_ge(w_used, out_units[o - ACTS] + 1)
                return opT[:, o % ACTS, 0, :, :]

            def operand_high(o, ready, count):
                act.wait_ge(ready, count)
                nc.scalar.activation(operand(o), conv[:, o % 2, :, :], ACT.Copy).then_inc(op_high, 1)

            act.wait_ge(par_landed, 16 * n_par_dmas)
            for j in range(n_ssd):
                ins = nc.scalar.activation(a_neg[:, j, :], a_neg[:, j, :], ACT.Exp)
            ins.then_inc(a_done, 1)

            for s, (kind, j, names) in enumerate(subs):
                for t in range(NT):
                    split_to(last_unit[s - 1] + 1 + t if s else 1)
                    for half in range(2):
                        act.wait_ge(xt_turned, 4 * s + 2 * t + half + 1)
                        bank = inner_of[("xt", s, t, half)]
                        nc.scalar.activation(xT[:, 4 * half:4 * half + 4, 0, t * P:(t + 1) * P],
                                             bank[:, :].rearrange("p (k c) -> p k c", k=4), ACT.Copy).then_inc(xt_high, 1)
                if kind == "ffn":
                    blocks = FFN // COLS
                    for b in range(blocks + 1):
                        if b < blocks:
                            o = n["op"] + b
                            bank = result(names[("fi", b)])
                            if o >= 2:
                                act.wait_ge(op_low, o - 1)
                            nc.scalar.activation(conv[:, o % 2, :, :], views(bank[:, :]), ACT.Relu).then_inc(relu_done, 1)
                        if b >= 1:
                            split_to(names[("fi", min(b + 1, blocks - 1))] + 2)
                            m = n["mlp"]
                            n["mlp"] += 1
                            o = n["op"] + b - 1
                            if b > HEAD_UNITS:
                                operand_high(o, square_done, m + 1)
                            else:
                                n["turned"] += 1
                                act.wait_ge(op_turned, n["turned"])
                                nc.scalar.activation(operand(o), views(inner_of[("op", o)][:, :]), ACT.Copy).then_inc(op_high, 1)
                    n["op"] += blocks
                elif kind == "ssd":
                    n0 = n["grp"]
                    n["grp"] += G
                    mixer = n0 // G

                    def start_conv(kind, g):
                        c = n["conv"]
                        n["conv"] += 1
                        bank = result(names[(kind, g)])
                        if c >= 2:
                            act.wait_ge(taps_done, 2 * (c - 1))
                        nc.scalar.activation(pad[:, c % 2, :, 2:2 + SEQ], views(bank[:, :]), ACT.Copy).then_inc(pad_filled, 1)
                        act.wait_ge(pad_filled, c + 1)
                        if c >= 2:
                            act.wait_ge(silu_done, 3 * ((c - 2) // 2) + (3 if c % 2 else 2))
                        for q, ct in enumerate(channel_tiles(kind, g)):
                            nc.scalar.activation(conv[:, c % 2, q, :], pad[:, c % 2, q, 0:SEQ], ACT.Identity,
                                                 bias=tap(j, TAPS, ct), scale=tap(j, 0, ct)).then_inc(first_tap, 1)

                    def tanh_of(src, scale):
                        m = n["th"]
                        n["th"] += 1
                        if m >= 2:
                            act.wait_ge(silu_done, m - 1)
                        nc.scalar.activation(th[:, m % 2, :], src, ACT.Tanh, scale=scale).then_inc(tanh_done, 1)

                    def conv_tanh():
                        c = n["conv"] - 1
                        act.wait_ge(taps_done, 2 * (c + 1))
                        tanh_of(conv[:, c % 2, :, :].rearrange("p a b -> p (a b)"), 1.0)

                    act.wait_ge(par_done, 2 * n_ssd + 1)
                    for i in range(G + 3):
                        if i < G:
                            bank = result(names[("z", i)])
                            tanh_of(bank[:, :], 0.5)
                        if i == 0:
                            split_to(names[("dt", 0)] + 3)
                            act.wait_ge(dt_biased, mixer + 1)
                            nc.scalar.activation(dtt[:, 1, :, :], dtt[:, 0, :, :], ACT.Abs).then_inc(act_step, 1)
                            n["step"] += 1
                            act.wait_ge(act_step, n["step"])
                            nc.scalar.activation(dtt[:, 2, :, :], dtt[:, 1, :, :], ACT.Exp, scale=-1.0).then_inc(dt_exp, 1)
                        if 1 <= i <= G:
                            m = n0 + i - 1
                            act.wait_ge(xs_turned, m + 1)
                            if m >= 3:
                                act.wait_ge(gated, m - 2)
                            nc.scalar.activation(tri_b[:, m % 3, :], inner_of[("xs", m)][:, :], ACT.Copy).then_inc(xs_copied, 1)
                        if i >= 3:
                            g = i - 3
                            o = n["op"]
                            n["op"] += 1
                            n["turned"] += 1
                            act.wait_ge(op_turned, n["turned"])
                            dst = operand(o)
                            for c in range(2):
                                ins = nc.scalar.activation(dst[:, c, :], inner_of[("op", o)][:, c * SEQ:(c + 1) * SEQ],
                                                           ACT.Copy, scale=tap(j, TAPS + 1, 2 * g + c))
                            ins.then_inc(op_high, 1)
                        if i < G:
                            start_conv("bc", i)
                            conv_tanh()
                        if i == 0:
                            act.wait_ge(cs_copied, mixer + 1)
                            nc.scalar.activation(ncs[:, :, :], inner_of[("cs", j)][:, 0:NT * 2 * HEADS]
                                                 .rearrange("p (t c) -> p t c", t=NT), ACT.Copy,
                                                 scale=-1.0).then_inc(ncs_done, 1)
                        if i < G:
                            start_conv("x", i)
                            conv_tanh()
                        if i == 0:
                            act.wait_ge(cs_rows, mixer + 1)
                            act.dma_start(rows_dram[j], csT[:, :]).then_inc(rows_stored, 16)
                            act.wait_ge(ncs_done, mixer + 1)
                        if 1 <= i <= G:
                            g, m = i - 1, n0 + i - 1
                            act.wait_ge(e_masked, m + 1)
                            for h in range(HPG):
                                for q, (off, width) in enumerate(E_PART):
                                    col = (HEADS if q in (1, 2) else 0) + g * HPG + h
                                    e = E[:, m % 2, h * E_HEAD + off:h * E_HEAD + off + width]
                                    ins = nc.scalar.activation(e, e, ACT.Exp, bias=ncs[:, q // 2, col:col + 1])
                            ins.then_inc(e_exp, 1)
                        if 2 <= i < G + 2:
                            m = n0 + i - 2
                            act.wait_ge(gated, m + 1)
                            if m:
                                act.wait_ge(rms_done, m)
                            for t in range(NT):
                                ins = nc.scalar.activation(sq[:, t * GW:(t + 1) * GW], gate[:, t * GW:(t + 1) * GW],
                                                           ACT.Square, accum_out=small[:, 4 + t:5 + t])
                            ins.then_inc(msq_done, 1)
                            if i < G:
                                split_to(names[("x", i)] + 3)
                            act.wait_ge(rms_done, m + 1)
                            for t in range(NT):
                                v = gate[:, t * GW:(t + 1) * GW]
                                ins = nc.scalar.activation(v, v, ACT.Copy, scale=small[:, 8 + t:9 + t])
                            ins.then_inc(scaled, 1)
                elif kind == "conv":
                    for b in range(5):
                        if b < 4:
                            bank = result(names[("cc", b)])
                            if b >= 2:
                                act.wait_ge(sc_prod, b - 1)
                            nc.scalar.activation(th[:, b % 2, :], bank[:, :], ACT.Copy).then_inc(sc_c, 1)
                        if b >= 1:
                            split_to(names[("cb", b - 1)] + 3)
                            operand_high(n["op"], sc_gated, b)
                            n["op"] += 1
                else:
                    def keep_qkv(k, b):
                        bank = result(names[("vqk"[k], b)])
                        if b == 3:
                            act.wait_ge(o_ready, BLOCK_HEADS)
                        dst = (tri_c, tri_a, tri_b)[k]
                        src = reversed_rows(bank) if k == 1 else bank[:, :]
                        out = dst[:, b % 3, :].rearrange("p (a c) -> p a c", c=GRID_W) if k == 1 else dst[:, b % 3, :]
                        nc.scalar.activation(out, src, ACT.Copy).then_inc(qkv_done, 1)

                    def scale_out(h):
                        blk, hh = h // BLOCK_HEADS, h % BLOCK_HEADS
                        act.wait_ge(o_ready, h + 1)
                        act.wait_ge(p_scale, h + 1)
                        if blk >= 2 and hh == 0:
                            act.wait_ge(op_turned, n["turned"] - (1 if n["turned"] > base + blk - 1 else 0))
                        for t in range(NT):
                            c = t * COLS + hh * NAD
                            ins = nc.scalar.activation(o_b[blk % 2][:, c:c + NAD], inner_of[("o", h)][:, t * NAD:(t + 1) * NAD],
                                                       ACT.Copy, scale=att[:, h % 2, 6 + t:7 + t])
                        ins.then_inc(o_done, 1)

                    base = n["turned"]
                    for b in range(6):
                        for k in range(4):
                            h = 4 * (b - 1) + k
                            if 0 <= h < NAH:
                                act.wait_ge(s_max, h + 1)
                                for t in range(NT):
                                    v = prob_b[h % 2][:, t * SEQ:(t + 1) * SEQ]
                                    ins = nc.scalar.activation(v, v, ACT.Exp, bias=att[:, h % 2, 2 + t:3 + t],
                                                               accum_out=att[:, h % 2, 4 + t:5 + t])
                                ins.then_inc(p_done, 1)
                            if k < 3 and b < 4:
                                keep_qkv(k, b)
                            if 1 <= h <= NAH:
                                scale_out(h - 1)
                            if 0 <= h < NAH:
                                act.wait_ge(pt_ready, h + 1)
                                nc.scalar.activation(probT_b[h % 2], inner_of[("pt", h)][:, :], ACT.Copy).then_inc(pt_done, 1)
                            if k == 1 and b >= 2:
                                o = n["op"]
                                n["op"] += 1
                                n["turned"] += 1
                                act.wait_ge(op_turned, n["turned"])
                                nc.scalar.activation(grid_rows(operand(o)), reversed_rows(inner_of[("op", o)]),
                                                     ACT.Copy).then_inc(op_high, 1)

            split_to(len(units) - 1)

        @block.vector
        def _(dve):
            n = dict.fromkeys(["split", "step", "op", "turned", "grp", "conv", "th", "mlp"], 0)
            V = nc.vector

            def step(ins):
                ins.then_inc(dve_step, 1)
                n["step"] += 1
                return n["step"]

            def after(count):
                dve.wait_ge(dve_step, count)

            def chain(ins):
                after(step(ins))

            def split_to(last):
                while n["split"] <= min(last, len(units) - 1):
                    u = n["split"]
                    n["split"] += 1
                    _, k, c = weight_parts(u)
                    dve.wait_ge(raw_landed[u % RAW], 32 * (u // RAW + 1))
                    dve.wait_ge(w_high_done, u + 1)
                    if u >= SPLIT:
                        dve.wait_ge(w_used, u - SPLIT + 1)
                    V.tensor_tensor(w_low[:, u % SPLIT, 0:k * c], raw[:, u % RAW, 0:k * c],
                                    f(w_high[:, u % SPLIT, 0:k * c]), ALU.subtract).then_inc(w_low_done, 1)

            def result(u):
                split_to(u + 3)
                dve.wait_ge(w_used, u + 1)
                return acc_of[u]

            def operand(o):
                if o >= ACTS:
                    dve.wait_ge(w_used, out_units[o - ACTS] + 1)
                return opT[:, o % ACTS, 1, :, :], f(opT[:, o % ACTS, 0, :, :])

            def operand_low(o, src):
                dve.wait_ge(op_high, o + 1)
                low, high = operand(o)
                V.tensor_tensor(low, src, high, ALU.subtract).then_inc(op_low, 1)

            def norm(s, t):
                split_to(last_unit[s] + 1 + t)
                if t == 0:
                    dve.wait_ge(y_ready, s + 1)
                else:
                    dve.wait_ge(w_used, last_unit[s] + 1)
                halves = [xs[:, t, c * 512:(c + 1) * 512] for c in range(2)]
                a = step(V.scalar_tensor_tensor(out=halves[0], in0=halves[0], scalar=ALPHA, in1=Y[t][0][:, :],
                                                op0=ALU.mult, op1=ALU.add))
                V.scalar_tensor_tensor(out=halves[1], in0=halves[1], scalar=ALPHA, in1=Y[t][1][:, :],
                                       op0=ALU.mult, op1=ALU.add).then_inc(y_free, 1)
                after(a)
                V.bn_stats(stats[:, 0, :], halves[0])
                dve.wait_ge(y_free, 2 * s + t + 1)
                chain(V.bn_stats(stats[:, 1, :], halves[1]))
                chain(V.bn_aggr(mv[:, :], stats[:, :, :]))
                V.tensor_scalar(small[:, t:t + 1], mv[:, 1:2], EPS, None, ALU.add).then_inc(var_done, 1)
                dve.wait_ge(gb_landed, 32 * (s + 1))
                cents = []
                for c in range(2):
                    cents.append(step(V.scalar_tensor_tensor(out=halves[c], in0=halves[c], scalar=mv[:, 0:1],
                                                             in1=gb[:, 0, c * 512:(c + 1) * 512],
                                                             op0=ALU.subtract, op1=ALU.mult)))
                dve.wait_ge(rstd_done, 2 * s + t + 1)
                for c in range(2):
                    after(cents[c])
                    V.scalar_tensor_tensor(out=halves[c], in0=halves[c], scalar=small[:, 2 + t:3 + t],
                                           in1=gb[:, 1, c * 512:(c + 1) * 512],
                                           op0=ALU.mult, op1=ALU.add).then_inc(ln_out, 1)

            dve.wait_ge(x_landed, 16 * NT)
            for j in range(n_ssd):
                dve.wait_ge(par_turned, j + 1)
                bank = inner_of[("par", j)]
                V.tensor_scalar(ssd_par[:, j, 0:TAPS + 1, :], bank[:, 0:(TAPS + 1) * CT]
                                .rearrange("p (a b) -> p a b", b=CT), 0.5, None, ALU.mult).then_inc(par_done, 1)
                V.tensor_copy(ssd_par[:, j, TAPS + 1, 0:DI // P],
                              bank[:, (TAPS + 1) * CT:(TAPS + 1) * CT + DI // P]).then_inc(par_done, 1)
            dve.wait_ge(par_turned, n_ssd + 1)
            V.tensor_copy(sc_par[:, :, :], inner_of[("par", n_ssd)][:, 0:SC_TAPS * KT]
                          .rearrange("p (a b) -> p a b", b=KT)).then_inc(par_done, 1)
            dve.wait_ge(par_done, 2 * n_ssd + 1)
            dve.wait_ge(a_done, 1)

            for s, (kind, j, names) in enumerate(subs):
                for t in range(NT):
                    if s:
                        norm(s - 1, t)
                    else:
                        split_to(1)
                    for half in range(2):
                        m = 4 * s + 2 * t + half + 1
                        dve.wait_ge(xt_high, m)
                        dst = xT[:, 4 * half:4 * half + 4, :, t * P:(t + 1) * P]
                        V.tensor_tensor(dst[:, :, 1, :], inner_of[("xt", s, t, half)][:, :].rearrange("p (k c) -> p k c", k=4),
                                        f(dst[:, :, 0, :]), ALU.subtract).then_inc(xt_low, 1)
                if kind == "ffn":
                    def turned_low(o):
                        dve.wait_ge(op_turned, n["turned"] + 1)
                        n["turned"] += 1
                        operand_low(o, views(inner_of[("op", o)][:, :]))

                    for b in range(FFN // COLS):
                        o = n["op"]
                        n["op"] += 1
                        m = n["mlp"]
                        n["mlp"] += 1
                        result(names[("fi", b)])
                        dve.wait_ge(relu_done, m + 1)
                        V.tensor_tensor(conv[:, o % 2, :, :], conv[:, o % 2, :, :], conv[:, o % 2, :, :],
                                        ALU.mult).then_inc(square_done, 1)
                        if b + 1 < FFN // COLS:
                            split_to(names[("fi", b + 1)] + 2)
                        if 1 <= b <= HEAD_UNITS:
                            turned_low(o - 1)
                        if b >= HEAD_UNITS:
                            dve.wait_ge(square_done, m + 1)
                            operand_low(o, conv[:, o % 2, :, :])
                elif kind == "ssd":
                    n0 = n["grp"]
                    n["grp"] += G
                    mixer = n0 // G

                    def time_constants():
                        bank = result(names[("dt", 0)])
                        cols = 2 * HEADS
                        V.tensor_tensor(dtt[:, 0, :, :], bank[:, 0:NT * cols].rearrange("p (t c) -> p t c", t=NT),
                                        spread(dt_bias[:, j, :], [[0, NT], [1, cols]]), ALU.add).then_inc(dt_biased, 1)
                        dve.wait_ge(dt_exp, mixer + 1)
                        v, w1, e, r, r2, a = (dtt[:, q, :, :] for q in range(6))
                        chain(V.tensor_scalar(w1, e, 2.0, None, ALU.add))
                        chain(V.reciprocal(w1, w1))
                        chain(V.tensor_tensor(r, e, w1, ALU.mult))
                        chain(V.tensor_tensor(r2, r, r, ALU.mult))
                        chain(V.tensor_scalar(e, r2, 1.0 / 15, None, ALU.mult))
                        for q in (13, 11, 9, 7, 5, 3):
                            chain(V.scalar_tensor_tensor(out=e, in0=e, scalar=1.0 / q, in1=r2, op0=ALU.add, op1=ALU.mult))
                        chain(V.scalar_tensor_tensor(out=e, in0=e, scalar=1.0, in1=r, op0=ALU.add, op1=ALU.mult))
                        chain(V.tensor_scalar(w1, v, 0.0, None, ALU.max))
                        chain(V.scalar_tensor_tensor(out=dts[:, :, :], in0=e, scalar=2.0, in1=w1, op0=ALU.mult, op1=ALU.add))
                        V.scalar_tensor_tensor(out=a, in0=dts[:, :, :], scalar=-1.0,
                                               in1=spread(a_neg[:, j, :], [[0, NT], [1, cols]]),
                                               op0=ALU.mult, op1=ALU.mult).then_inc(a_steps, 1)

                    def taps(kind, g):
                        c = n["conv"]
                        n["conv"] += 1
                        split_to(names[(kind, g)] + 3)
                        dve.wait_ge(first_tap, 2 * (c + 1))
                        done = [0, 0]
                        for q in range(1, TAPS):
                            for i, ct in enumerate(channel_tiles(kind, g)):
                                if q > 1:
                                    after(done[i])
                                y = conv[:, c % 2, i, :]
                                ins = V.scalar_tensor_tensor(out=y, in0=pad[:, c % 2, i, q:q + SEQ], scalar=tap(j, q, ct),
                                                             in1=y, op0=ALU.mult, op1=ALU.add)
                                if q < TAPS - 1:
                                    done[i] = step(ins)
                                else:
                                    ins.then_inc(taps_done, 1)
                        return conv[:, c % 2, :, :].rearrange("p a b -> p (a b)")

                    def silu(dst, half_y):
                        m = n["th"]
                        n["th"] += 1
                        dve.wait_ge(tanh_done, m + 1)
                        V.scalar_tensor_tensor(out=dst, in0=th[:, m % 2, :], scalar=1.0, in1=half_y,
                                               op0=ALU.add, op1=ALU.mult).then_inc(silu_done, 1)

                    for i in range(G + 3):
                        if i < G:
                            m = n0 + i
                            bank = result(names[("z", i)])
                            if m >= 3:
                                dve.wait_ge(gated, m - 2)
                            silu(tri_c[:, m % 3, :], bank[:, :])
                        if i == 0:
                            time_constants()
                        if i >= 3:
                            g = i - 3
                            o = n["op"]
                            n["op"] += 1
                            dve.wait_ge(op_high, o + 1)
                            low, high = operand(o)
                            for c in range(2):
                                ins = V.scalar_tensor_tensor(out=low[:, c, :], in0=inner_of[("op", o)][:, c * SEQ:(c + 1) * SEQ],
                                                             scalar=tap(j, TAPS + 1, 2 * g + c), in1=high[:, c, :],
                                                             op0=ALU.mult, op1=ALU.subtract)
                            ins.then_inc(op_low, 1)
                        if 2 <= i < G + 2:
                            g, m = i - 2, n0 + i - 2
                            dve.wait_ge(cb_ready, m + 1)
                            dve.wait_ge(e_exp, m + 1)
                            cb = inner_of[("cb", m)]
                            for h in range(HPG):
                                for q, (off, width) in enumerate(E_PART):
                                    col = (HEADS if q in (1, 2) else 0) + g * HPG + h
                                    l0 = (q // 2) * SEQ + (P if q == 3 else 0)
                                    v = E[:, m % 2, h * E_HEAD + off:h * E_HEAD + off + width]
                                    ins = V.scalar_tensor_tensor(out=v, in0=v, scalar=dts[:, q // 2, col:col + 1],
                                                                 in1=cb[:, l0:l0 + width], op0=ALU.mult, op1=ALU.mult)
                            ins.then_inc(g_done, 1)
                        if i < G:
                            m = n0 + i
                            y = taps("bc", i)
                            if m >= 3:
                                dve.wait_ge(cb_ready, m - 2)
                            silu(tri_a[:, m % 3, :], y)
                        if i == 0:
                            dve.wait_ge(cs_acc, mixer + 1)
                            V.tensor_copy(cs[:, :, :], inner_of[("cs", j)][:, 0:NT * 2 * HEADS]
                                          .rearrange("p (t c) -> p t c", t=NT)).then_inc(cs_copied, 1)
                        if i < G:
                            y = taps("x", i)
                            if m >= 2:
                                dve.wait_ge(xs_turned, m - 1)
                            silu(xsT[:, m % 2, :, :].rearrange("p a b -> p (a b)"), y)
                        if i == 0:
                            dve.wait_ge(cs_turned, mixer + 1)
                            V.tensor_copy(csT[:, :], inner_of[("cs_rows", j)][0:2 * HEADS, 0:SEQ]).then_inc(cs_rows, 1)
                        if 2 <= i < G + 2:
                            g, m = i - 2, n0 + i - 2
                            dve.wait_ge(xs_copied, m + 1)
                            if m > n0:
                                dve.wait_ge(op_turned, n["turned"] + 1)
                                n["turned"] += 1
                            shape = [[GW, NT], [HD, HPG], [1, HD]]
                            chain(V.tensor_tensor(spread(gate[:, :], shape), spread(tri_b[:, m % 3, :], shape),
                                                  spread(skip[:, j, g * HPG:(g + 1) * HPG], [[0, NT], [1, HPG], [0, HD]]),
                                                  ALU.mult))
                            dve.wait_ge(yg_ready, m + 1)
                            V.tensor_tensor(gate[:, :], gate[:, :], inner_of[("yg", m)][:, :], ALU.add).then_inc(y_added, 1)
                            dve.wait_ge(y_added, m + 1)
                            V.scalar_tensor_tensor(out=gate[:, :], in0=gate[:, :], scalar=0.5, in1=tri_c[:, m % 3, :],
                                                   op0=ALU.mult, op1=ALU.mult).then_inc(gated, 1)
                    n["turned"] += 1
                elif kind == "conv":
                    for b in range(4):
                        o = n["op"]
                        n["op"] += 1
                        bank = result(names[("ch", b)])
                        dve.wait_ge(sc_c, b + 1)
                        V.tensor_tensor(pad[:, b % 2, :, 2:2 + SEQ], views(th[:, b % 2, :]), views(bank[:, :]),
                                        ALU.mult).then_inc(sc_prod, 1)
                        dve.wait_ge(sc_prod, b + 1)
                        if o >= 2:
                            dve.wait_ge(op_high, o - 1)
                            dve.wait_ge(op_low, o - 1)
                        done = [0, 0]
                        for q in range(SC_TAPS):
                            for i in range(2):
                                ct = 2 * b + i
                                y, src, w = conv[:, o % 2, i, :], pad[:, b % 2, i, 1 + q:1 + q + SEQ], sc_par[:, q, ct:ct + 1]
                                if q:
                                    after(done[i])
                                    done[i] = step(V.scalar_tensor_tensor(out=y, in0=src, scalar=w, in1=y,
                                                                          op0=ALU.mult, op1=ALU.add))
                                else:
                                    done[i] = step(V.tensor_scalar(y, src, w, None, ALU.mult))
                        bank = result(names[("cb", b)])
                        after(done[1])
                        V.tensor_tensor(conv[:, o % 2, :, :], conv[:, o % 2, :, :], views(bank[:, :]),
                                        ALU.mult).then_inc(sc_gated, 1)
                        dve.wait_ge(sc_gated, b + 1)
                        operand_low(o, conv[:, o % 2, :, :])
                else:
                    for b in range(6):
                        for k in range(4):
                            h = 4 * (b - 1) + k
                            if 0 <= h < NAH:
                                p, st = prob_b[h % 2], att[:, h % 2, :]
                                dve.wait_ge(s_ready, h + 1)
                                dve.wait_ge(bias_masked, h + 1)
                                if h >= 2:
                                    dve.wait_ge(pt_ready, h - 1)
                                    dve.wait_ge(o_done, h - 1)
                                V.scalar_tensor_tensor(out=p, in0=inner_of[("s", h)][:, :], scalar=float(NAD) ** -0.5,
                                                       in1=bias_b[h % 4], op0=ALU.mult, op1=ALU.add).then_inc(s_biased, 1)
                                dve.wait_ge(s_biased, h + 1)
                                chain(V.tensor_reduce(st[:, 0:2], views(p), AX.X, ALU.max))
                                V.tensor_scalar(st[:, 2:4], st[:, 0:2], -1.0, None, ALU.mult).then_inc(s_max, 1)
                            if k < 3 and b < 4:
                                split_to(names[("vqk"[k], b)] + 3)
                            if 0 <= h < NAH:
                                dve.wait_ge(p_done, h + 1)
                                V.reciprocal(st[:, 6:8], st[:, 4:6]).then_inc(p_scale, 1)
                            if k == 1 and b >= 2:
                                o = n["op"]
                                n["op"] += 1
                                n["turned"] += 1
                                dve.wait_ge(op_high, o + 1)
                                low, high = operand(o)
                                V.tensor_tensor(grid_rows(low), reversed_rows(inner_of[("op", o)]), grid_rows(high),
                                                ALU.subtract).then_inc(op_low, 1)
            for t in range(NT):
                norm(len(subs) - 1, t)


_INS = ["x", "ln_mix_g", "ln_mix_b", "ln_ffn_g", "ln_ffn_b", "ffn_w_in", "ffn_w_out", "ssd_w_in", "ssd_conv_w",
        "ssd_conv_b", "ssd_dt_bias", "ssd_a_log", "ssd_d", "ssd_norm_w", "ssd_w_out", "sc_w_in", "sc_conv_w",
        "sc_w_out", "na_w_qkv", "na_rpb", "na_w_out"]


def kernel(**inputs):
    import numpy as np
    import concourse.bacc as bacc
    from concourse.bass_utils import run_bass_kernel_spmd

    nc = bacc.Bacc("TRN2", target_bir_lowering=False, num_devices=1)
    arrays, args = {}, []
    for name in _INS:
        a = np.ascontiguousarray(inputs[name])
        arrays[f"in_{name}"] = a
        args.append(nc.dram_tensor(f"in_{name}", a.shape, mybir.dt.from_np(a.dtype), kind="ExternalInput").ap())
    args.append(nc.dram_tensor("out_x", (1, SEQ, D), F32, kind="ExternalOutput").ap())
    build(nc, *args)
    r = run_bass_kernel_spmd(nc, [arrays], core_ids=[0])
    return r.results[0]["out_x"]
```

```python
from contextlib import ExitStack

import concourse.bass as bass
from concourse import mybir

F32 = mybir.dt.float32
F32R = mybir.dt.float32r
ALU = mybir.AluOpType
ACT = mybir.ActivationFunctionType
AX = mybir.AxisListType

P = 128
D = 1024
SEQ = 256
NT = SEQ // P
KT = D // P
DEPTH = 4
ALPHA = (2.0 * DEPTH) ** 0.25
EPS = 1e-5
FFN = 4 * D

DI = 2 * D
HD = 64
HEADS = DI // HD
G = 8
NST = 128
HPG = HEADS // G
TAPS = 5
CONV_DIM = DI + 2 * G * NST
CT = CONV_DIM // P
GW = DI // G

SC_TAPS = 3

GRID_W = 64
ROWS = SEQ // GRID_W
NAH = 16
NAD = D // NAH
WIN_R, WIN_C = 8, 16
RPB_R, RPB_C = 2 * WIN_R - 1, 2 * WIN_C - 1
BLOCK_HEADS = 4

UNIT = 2048
COLS = UNIT // KT
RAW = 3
SPLIT = 4
ACTS = 4
HEAD_UNITS = 3
MLP_LAG = 4
AHEAD_OF_NORM = {"ffn": (0, 1), "ssd": (2, 3), "conv": (2, 3), "attn": (2, 3)}
E_HEAD = 768
E_PART = [(0, 256), (256, 128), (384, 256), (640, 128)]
GONE = -3.0e38

LAYERS = [("ssd", 0), ("conv", 0), ("attn", 0), ("ssd", 1)]


def plan_units(layers):
    units, subs = [], []

    def add(names, kind, j, b):
        names[(kind, b)] = len(units)
        units.append((kind, j, b))

    for i, (kind, j) in enumerate(layers):
        names = {}
        if kind == "ssd":
            for g in range(G + 2):
                if g < G - 1:
                    add(names, "z", j, g)
                if g == 0:
                    add(names, "dt", j, 0)
                if g < G:
                    add(names, "bc", j, g)
                    add(names, "x", j, g)
                if g == G - 1:
                    add(names, "z", j, g)
                if g >= 2:
                    add(names, "so", j, g - 2)
        elif kind == "conv":
            for b in range(5):
                if b < 4:
                    for what in ("cc", "ch", "cb"):
                        add(names, what, j, b)
                if b >= 1:
                    add(names, "co", j, b - 1)
        else:
            for b in range(4):
                for what in ("v", "q", "k"):
                    add(names, what, j, b)
            for b in range(4):
                add(names, "no", j, b)
        subs.append((kind, j, names))
        names = {}
        for b in range(FFN // COLS + MLP_LAG):
            if b < FFN // COLS:
                add(names, "fi", i, b)
            if b >= MLP_LAG:
                add(names, "fo", i, b - MLP_LAG)
        subs.append(("ffn", i, names))
    return units, subs


def silu_count(kind, m):
    order = ("bc", "x", "z") if m % G == G - 1 else ("z", "bc", "x")
    return 3 * m + 1 + order.index(kind)


def build(nc, x, ln_mix_g, ln_mix_b, ln_ffn_g, ln_ffn_b, ffn_w_in, ffn_w_out, ssd_w_in, ssd_conv_w,
          ssd_conv_b, ssd_dt_bias, ssd_a_log, ssd_d, ssd_norm_w, ssd_w_out, sc_w_in, sc_conv_w,
          sc_w_out, na_w_qkv, na_rpb, na_w_out, out):
    units, subs = plan_units(LAYERS)
    n_ssd = ssd_w_in.shape[0]

    def weight_parts(u):
        kind, j, b = units[u]

        def cols(w, c0, n):
            return w[j].rearrange("(k p) n -> p k n", p=P)[:, :, c0:c0 + n]

        if kind == "dt":
            return [(cols(ssd_w_in, DI + CONV_DIM, 2 * HEADS), 0, 2 * HEADS)], KT, 2 * HEADS
        if kind == "bc":
            return [(cols(ssd_w_in, 2 * DI + b * NST, NST), 0, NST),
                    (cols(ssd_w_in, 2 * DI + (G + b) * NST, NST), NST, 2 * NST)], KT, COLS
        start = {"x": (ssd_w_in, DI), "z": (ssd_w_in, 0), "fi": (ffn_w_in, 0),
                 "cb": (sc_w_in, 0), "cc": (sc_w_in, D), "ch": (sc_w_in, 2 * D),
                 "q": (na_w_qkv, 0), "k": (na_w_qkv, D), "v": (na_w_qkv, 2 * D)}
        if kind in start:
            w, c0 = start[kind]
            return [(cols(w, c0 + b * COLS, COLS), 0, COLS)], KT, COLS
        w = {"so": ssd_w_out, "co": sc_w_out, "no": na_w_out, "fo": ffn_w_out}[kind]
        return [(w[j].rearrange("(k p) n -> p k n", p=P)[:, 2 * b:2 * b + 2, :], 0, D)], 2, D

    with ExitStack() as ctx:
        def sb(name, shape, dt=F32):
            return ctx.enter_context(nc.sbuf_tensor(name, shape, dt))

        def sem(name):
            return ctx.enter_context(nc.semaphore(name))

        raw = sb("raw", [P, RAW, UNIT])
        w_high = sb("w_high", [P, SPLIT, UNIT], F32R)
        w_low = sb("w_low", [P, SPLIT, UNIT], F32R)
        xT = sb("xT", [P, KT, 2, SEQ], F32R)
        opT = sb("opT", [P, ACTS, 2, 2, SEQ], F32R)
        xs = sb("x_tokens", [P, NT, D])
        gb = sb("ln_gain_bias", [P, 2, D])
        E = sb("E", [P, 2, HPG * E_HEAD])
        ssd_rows = E[0:CT, 0, 0:n_ssd * (TAPS + 2) * P].rearrange("c (j q p) -> c j q p", j=n_ssd, p=P)
        sc_rows = E[0:KT, 1, 0:SC_TAPS * P].rearrange("c (q p) -> c q p", p=P)
        tri_a = sb("ring_a", [P, 3, 512])
        tri_b = sb("ring_b", [P, 3, 512])
        tri_c = sb("ring_c", [P, 3, 512])
        pad = sb("conv_pad", [P, 2, 2, SEQ + TAPS - 1])
        conv = sb("conv", [P, 2, 2, SEQ])
        th = sb("tanh", [P, 2, 512])
        xsT = sb("xsT", [P, 2, 2, SEQ])
        gate = sb("gate", [P, 512])
        sq = sb("square", [P, 512])
        ident = sb("ident", [P, P])
        ones = sb("ones", [P, P])
        prefix = sb("prefix", [P, P])
        suffix = sb("suffix", [P, P])
        ssd_par = sb("ssd_par", [P, n_ssd, TAPS + 2, CT])
        sc_par = sb("sc_par", [P, SC_TAPS, KT])
        dt_bias = sb("dt_bias", [P, n_ssd, 2 * HEADS])
        a_neg = sb("a_neg", [P, n_ssd, 2 * HEADS])
        skip = sb("skip", [P, n_ssd, HEADS])
        dts = sb("dts", [P, NT, 2 * HEADS])
        dtt = xsT[:, :, :, :].rearrange("p a b c -> p (a b c)")[:, 0:6 * NT * 2 * HEADS].rearrange(
            "p (q t c) -> p q t c", q=6, t=NT)
        cs = sb("cumsum", [P, NT, 2 * HEADS])
        ncs = sb("neg_cumsum", [P, NT, 2 * HEADS])
        csT = sb("cumsum_rows", [2 * HEADS, SEQ])
        stats = sb("stats", [P, 2, 6])
        mv = sb("mean_var", [P, 2])
        small = sb("small", [P, 16])
        half_neg = sb("minus_half", [P, 2])
        att = sb("softmax_stats", [P, 2, 8])
        rows_dram = nc.dram_tensor("cumsum_dram", [n_ssd, 2 * HEADS, SEQ], F32, kind="Internal").ap()

        Y = [[ctx.enter_context(nc.psum_tensor(f"y{t}{n}", [P, 512], F32)) for n in range(2)] for t in range(NT)]
        A = [ctx.enter_context(nc.psum_tensor(f"acc{n}", [P, 512], F32)) for n in range(2)]
        I = [ctx.enter_context(nc.psum_tensor(f"inner{n}", [P, 512], F32)) for n in range(2)]

        raw_landed = [sem(f"raw_landed{n}") for n in range(RAW)]
        x_landed = [sem(f"x_landed{t}") for t in range(NT)]
        par_landed = [sem(f"par_landed{n}") for n in range(2)]
        gb_landed = sem("gb_landed")
        rows_stored = sem("rows_stored")
        e_landed = [sem(f"e_landed{n}") for n in range(2)]
        bias_landed = [sem(f"bias_landed{n}") for n in range(4)]
        out_stored = sem("out_stored")
        w_high_done, w_low_done, w_used = sem("w_high_done"), sem("w_low_done"), sem("w_used")
        consts, par_turned, par_done, a_done = sem("consts"), sem("par_turned"), sem("par_done"), sem("a_done")
        y_ready, y_free = sem("y_ready"), sem("y_free")
        var_done, rstd_done = sem("var_done"), sem("rstd_done")
        ln_out, xt_turned = sem("ln_out"), sem("xt_turned")
        xt_high, xt_low = sem("xt_high"), sem("xt_low")
        op_turned, op_high, op_low = sem("op_turned"), sem("op_high"), sem("op_low")
        relu_done, square_done = sem("relu_done"), sem("square_done")
        dt_biased, dt_exp = sem("dt_biased"), sem("dt_exp")
        a_steps, cs_acc, cs_copied, ncs_done = sem("a_steps"), sem("cs_acc"), sem("cs_copied"), sem("ncs_done")
        cs_turned, cs_rows = sem("cs_turned"), sem("cs_rows")
        pad_filled, first_tap, taps_done = sem("pad_filled"), sem("first_tap"), sem("taps_done")
        tanh_done, silu_done = sem("tanh_done"), sem("silu_done")
        xs_turned, xs_copied = sem("xs_turned"), sem("xs_copied")
        xs_scaled, xs_skip = sem("xs_scaled"), sem("xs_skip")
        e_masked, e_exp, cb_ready, g_done = sem("e_masked"), sem("e_exp"), sem("cb_ready"), sem("g_done")
        yg_ready, y_added, gated = sem("yg_ready"), sem("y_added"), sem("gated")
        msq_done, rms_done, scaled = sem("msq_done"), sem("rms_done"), sem("scaled")
        sc_c, sc_prod, sc_gated = sem("sc_c"), sem("sc_prod"), sem("sc_gated")
        qkv_done = sem("qkv_done")
        s_ready, s_biased, s_max, p_done = sem("s_ready"), sem("s_biased"), sem("s_max"), sem("p_done")
        pt_ready, pt_done, o_ready, o_done = sem("pt_ready"), sem("pt_done"), sem("o_ready"), sem("o_done")
        bias_masked, p_scale = sem("bias_masked"), sem("p_scale")
        act_step, dve_step, pool_step = sem("act_step"), sem("dve_step"), sem("pool_step")

        def f(ap):
            return ap.bitcast(F32)

        def spread(ap, dims):
            return bass.AP(ap.tensor, ap.offset, [list(ap.ap[0])] + dims)

        def views(base):
            return base.rearrange("p (a b) -> p a b", a=2)

        bias_b = [E[:, 0, n * 512:(n + 1) * 512] for n in range(4)]
        prob_b = [E[:, 0, (4 + n) * 512:(5 + n) * 512] for n in range(2)]
        probT_b = [E[:, 1, n * 512:(n + 1) * 512] for n in range(2)]
        o_b = [E[:, 1, (2 + n) * 512:(3 + n) * 512] for n in range(2)]

        xs_fwd, xs_bwd = tri_a[:, 2, :], tri_b[:, 2, :]

        n_par_dmas = (6, (n_ssd - 1) * 6 + 1)
        out_units = [u for u, (kind, _, _) in enumerate(units) if kind in ("so", "co", "no", "fo")]
        in_units = [u for u in range(len(units)) if u not in out_units]
        extra = [names[("fi", HEAD_UNITS - 1)] for kind, _, names in subs if kind == "ffn"]
        acc_of = {u: A[k % 2] for k, u in enumerate(u for u in in_units if u not in extra)}
        acc_of.update({u: Y[0][0] for u in extra})
        inner_of = {}
        last_unit = [max(names.values()) for _, _, names in subs]

        def ahead_of_norm(s, t):
            if t and s + 1 < len(subs) and subs[s + 1][0] == "ssd":
                return last_unit[s] + 2
            return last_unit[s] + AHEAD_OF_NORM[subs[s][0]][t]

        block = ctx.enter_context(nc.Block())

        def load_parameters(engine, j, landed):
            engine.dma_start(ssd_rows[:, j, 0:TAPS, :],
                             ssd_conv_w[j].rearrange("a (c p) -> c a p", p=P)).then_inc(landed, 16)
            engine.dma_start(ssd_rows[:, j, TAPS, :],
                             ssd_conv_b[j].rearrange("(c p) -> c p", p=P)).then_inc(landed, 16)
            engine.dma_start(ssd_rows[0:DI // P, j, TAPS + 1, :],
                             ssd_norm_w[j].rearrange("(c p) -> c p", p=P)).then_inc(landed, 16)
            engine.dma_start(dt_bias[:, j, :], ssd_dt_bias[j:j + 1].rearrange("a b c -> a (b c)")
                             .to_broadcast([P, 2 * HEADS])).then_inc(landed, 16)
            engine.dma_start(a_neg[:, j, :], ssd_a_log[j:j + 1].rearrange("a b c -> a (b c)")
                             .to_broadcast([P, 2 * HEADS])).then_inc(landed, 16)
            engine.dma_start(skip[:, j, :], ssd_d[j:j + 1].to_broadcast([P, HEADS])).then_inc(landed, 16)

        @block.sync
        def _(sp):
            for u in range(len(units)):
                if u < NT:
                    sp.dma_start(xs[:, u, :], x[0, u * P:(u + 1) * P, :]).then_inc(x_landed[u], 16)
                parts, k, n = weight_parts(u)
                if u >= RAW:
                    sp.wait_ge(w_high_done, u - RAW + 1)
                    sp.wait_ge(w_low_done, u - RAW + 1)
                dst = raw[:, u % RAW, 0:k * n].rearrange("p (k n) -> p k n", k=k)
                if len(parts) == 1:
                    src = parts[0][0]
                    sp.dma_start(dst[:, 0:k // 2, :], src[:, 0:k // 2, :]).then_inc(raw_landed[u % RAW], 16)
                    sp.dma_start(dst[:, k // 2:k, :], src[:, k // 2:k, :]).then_inc(raw_landed[u % RAW], 16)
                else:
                    for src, c0, c1 in parts:
                        sp.dma_start(dst[:, :, c0:c1], src).then_inc(raw_landed[u % RAW], 16)
            last = len(subs) - 1
            for t in range(NT):
                sp.wait_ge(ln_out, 4 * last + 2 * t + 2)
                sp.dma_start(out[0, t * P:(t + 1) * P, :], xs[:, t, :]).then_inc(out_stored, 16)
            sp.wait_ge(out_stored, 16 * NT)

        @block.gpsimd
        def _(pool):
            step = [0]

            def own(ins):
                ins.then_inc(pool_step, 1)
                step[0] += 1
                pool.wait_ge(pool_step, step[0])

            own(nc.gpsimd.memset(ident[:, :], 0.0))
            own(nc.gpsimd.affine_select(out=ident[:, :], in_=ident[:, :], compare_op=ALU.not_equal, fill=1.0,
                                        base=0, pattern=[[-1, P]], channel_multiplier=1))
            nc.gpsimd.memset(half_neg[:, :], -0.5).then_inc(consts, 1)
            for j in range(1, n_ssd):
                load_parameters(pool, j, par_landed[1])
            pool.dma_start(sc_rows[:, :, :], sc_conv_w[0].rearrange("a (c p) -> c a p", p=P)).then_inc(par_landed[1], 16)
            own(nc.gpsimd.memset(ones[:, :], 1.0))
            own(nc.gpsimd.affine_select(out=prefix[:, :], in_=ones[:, :], compare_op=ALU.is_ge, fill=0.0,
                                        base=0, pattern=[[1, P]], channel_multiplier=-1))
            own(nc.gpsimd.affine_select(out=suffix[:, :], in_=ones[:, :], compare_op=ALU.is_ge, fill=0.0,
                                        base=0, pattern=[[-1, P]], channel_multiplier=1))
            nc.gpsimd.memset(pad[:, :, :, :], 0.0).then_inc(consts, 1)
            pool.wait_ge(consts, 2)
            group = [0]
            head = [0]

            def load_gain_bias(s):
                g_src, b_src = (ln_ffn_g, ln_ffn_b) if s % 2 else (ln_mix_g, ln_mix_b)
                if s:
                    pool.wait_ge(ln_out, 4 * s)
                pool.dma_start(gb[:, 0, :], g_src[s // 2:s // 2 + 1, :].to_broadcast([P, D])).then_inc(gb_landed, 16)
                pool.dma_start(gb[:, 1, :], b_src[s // 2:s // 2 + 1, :].to_broadcast([P, D])).then_inc(gb_landed, 16)

            def ln_power(s):
                for t in range(NT):
                    pool.wait_ge(var_done, 2 * s + t + 1)
                    nc.gpsimd.tensor_tensor(small[:, 2 + t:3 + t], small[:, t:t + 1], half_neg[:, 0:1],
                                            ALU.pow).then_inc(rstd_done, 1)

            for s, (kind, j, names) in enumerate(subs):
                load_gain_bias(s)
                if kind == "ssd":
                    first = group[0]
                    rows = rows_dram[j]
                    pool.wait_ge(rows_stored, 16 * (first // G + 1))

                    def load_decays(g):
                        n = first + g
                        if n >= 2:
                            pool.wait_ge(yg_ready, n - 1)
                        slot = E[:, n % 2, :].rearrange("p (h e) -> p h e", h=HPG)
                        for q, (off, width) in enumerate(E_PART):
                            back = q in (1, 2)
                            l0 = P if q == 3 else 0
                            r0 = (HEADS if back else 0) + g * HPG
                            src = rows[r0:r0 + HPG, l0:l0 + width]
                            src = bass.AP(src.tensor, src.offset, [[0, P], [SEQ, HPG], [1, width]])
                            pool.dma_start(slot[:, :, off:off + width], src).then_inc(e_landed[n % 2], 16)

                    def mask_decays(g):
                        n = first + g
                        pool.wait_ge(e_landed[n % 2], 64 * (n // 2 + 1))
                        slot = E[:, n % 2, :].rearrange("p (h e) -> p h e", h=HPG)
                        for q, (off, sign) in enumerate(((0, 1), (256, -1), (384 + P, -1), (640, 1))):
                            v = slot[:, :, off:off + P]
                            ins = nc.gpsimd.affine_select(out=v, in_=v, compare_op=ALU.is_ge, fill=GONE, base=0,
                                                          pattern=[[0, HPG], [sign, P]], channel_multiplier=-sign)
                        ins.then_inc(e_masked, 1)

                    def times_heads(dst, n, factors):
                        shape = [[GW, NT], [HD, HPG], [1, HD]]
                        return nc.gpsimd.tensor_tensor(spread(dst, shape), spread(tri_b[:, n % 2, :], shape),
                                                       factors, ALU.mult)

                    def scale_xs(g):
                        n = first + g
                        pool.wait_ge(xs_copied, n + 1)
                        if n:
                            pool.wait_ge(yg_ready, n)
                        per_head = [[2 * HEADS, NT], [1, HPG], [0, HD]]
                        times_heads(xs_fwd, n, spread(dts[:, 0, g * HPG:(g + 1) * HPG], per_head))
                        c = HEADS + g * HPG
                        times_heads(xs_bwd, n, spread(dts[:, 0, c:c + HPG], per_head)).then_inc(xs_scaled, 1)

                    def skip_xs(g):
                        n = first + g
                        pool.wait_ge(xs_scaled, n + 1)
                        times_heads(tri_b[:, n % 2, :], n, spread(skip[:, j, g * HPG:(g + 1) * HPG],
                                                                  [[0, NT], [1, HPG], [0, HD]])).then_inc(xs_skip, 1)

                    def rms_power(g):
                        n = first + g
                        pool.wait_ge(msq_done, n + 1)
                        own(nc.gpsimd.tensor_scalar(small[:, 6:8], small[:, 4:6], 1.0 / GW, EPS, ALU.mult, ALU.add))
                        nc.gpsimd.tensor_tensor(small[:, 8:10], small[:, 6:8], half_neg[:, :], ALU.pow).then_inc(rms_done, 1)

                    for g in range(2):
                        load_decays(g)
                        mask_decays(g)
                    for g in range(G - 1):
                        scale_xs(g)
                        if g >= 1:
                            rms_power(g - 1)
                            load_decays(g + 1)
                        skip_xs(g)
                        if g >= 1:
                            mask_decays(g + 1)
                    scale_xs(G - 1)
                    rms_power(G - 2)
                    skip_xs(G - 1)
                    rms_power(G - 1)
                    group[0] += G
                if kind == "attn":
                    def mask_bias(h):
                        pool.wait_ge(bias_landed[h % 4], 16 * ROWS * (h // 4 + 1))
                        edge = GRID_W - WIN_C
                        for half in range(2):
                            v = bias_b[h % 4][64 * half:64 * half + 64, :].rearrange("p (a c) -> p a c", c=GRID_W)
                            own(nc.gpsimd.affine_select(out=v[:, :, 0:edge], in_=v[:, :, 0:edge], compare_op=ALU.is_ge,
                                                        fill=GONE, base=WIN_C // 2 - GRID_W + 1,
                                                        pattern=[[0, 2 * ROWS], [1, edge]], channel_multiplier=1))
                            ins = nc.gpsimd.affine_select(out=v[:, :, WIN_C:], in_=v[:, :, WIN_C:], compare_op=ALU.is_ge,
                                                          fill=GONE, base=GRID_W - 1 + WIN_C // 2 - 1 - WIN_C,
                                                          pattern=[[0, 2 * ROWS], [-1, edge]], channel_multiplier=-1)
                        ins.then_inc(bias_masked, 1)

                    for h in range(NAH):
                        if h >= 4:
                            pool.wait_ge(s_biased, h - 3)
                        if h == 0:
                            pool.wait_ge(par_turned, n_ssd + 1)
                            if s:
                                pool.wait_ge(ln_out, 4 * s)
                        for r in range(ROWS):
                            src = bass.AP(na_rpb.tensor, na_rpb.offset + (h * RPB_R + WIN_R - 1 - r) * RPB_C
                                          + WIN_C - GRID_W, [[1, GRID_W], [RPB_C, ROWS], [1, GRID_W]])
                            c0 = (r // 2) * SEQ
                            dst = bias_b[h % 4][64 * (r % 2):64 * (r % 2) + 64, c0:c0 + SEQ]
                            pool.dma_start(dst.rearrange("p (a b) -> p a b", a=ROWS), src).then_inc(bias_landed[h % 4], 16)
                        if h >= 1:
                            mask_bias(h - 1)
                    mask_bias(NAH - 1)
                ln_power(s)

        @block.tensor
        def _(pe):
            acc_freed = []
            inn_freed = []
            n = dict.fromkeys(["conv", "z", "mlp", "op", "grp", "sc", "qkv", "dt", "opu"], 0)

            def acc_bank(freed_by):
                k = len(acc_freed)
                if k >= 2:
                    pe.wait_ge(*acc_freed[k - 2])
                acc_freed.append(freed_by)
                return A[k % 2]

            def inner_bank(key, freed_by):
                k = len(inn_freed)
                inner_of[key] = I[k % 2]
                if k >= 2:
                    pe.wait_ge(*inn_freed[k - 2])
                inn_freed.append(freed_by)
                return I[k % 2]

            def weights(u):
                pe.wait_ge(w_high_done, u + 1)
                pe.wait_ge(w_low_done, u + 1)
                return w_high[:, u % SPLIT, :], w_low[:, u % SPLIT, :]

            def x_half(s, t, half):
                pe.wait_ge(xt_high, 4 * s + 2 * t + half + 1)
                pe.wait_ge(xt_low, 4 * s + 2 * t + half + 1)

            def features(u, bank, ts, arriving, cs=range(2)):
                wh, wl = weights(u)
                span = slice(ts[0] * P, (ts[-1] + 1) * P)
                for c in cs:
                    for k in range(KT):
                        if arriving and c == 0 and k % (KT // 2) == 0:
                            x_half(*arriving, k // (KT // 2))
                        col = k * COLS + c * P
                        for part, (w, low) in enumerate(((wh, 0), (wh, 1), (wl, 0))):
                            mm = nc.tensor.matmul(bank[:, c * SEQ:(c + 1) * SEQ][:, span], w[:, col:col + P],
                                                  xT[:, k, low, span], start=(k == 0 and part == 0),
                                                  stop=(k == KT - 1 and part == 2))
                return mm

            def tokens(u, bank, ts, arriving, width):
                wh, wl = weights(u)
                for t in ts:
                    for k in range(KT):
                        if arriving and k % (KT // 2) == 0:
                            x_half(*arriving, k // (KT // 2))
                        for part, (w, low) in enumerate(((wh, 0), (wh, 1), (wl, 0))):
                            mm = nc.tensor.matmul(bank[:, t * width:(t + 1) * width], xT[:, k, low, t * P:(t + 1) * P],
                                                  w[:, k * width:(k + 1) * width], start=(k == 0 and part == 0),
                                                  stop=(k == KT - 1 and part == 2))
                return mm

            def used(mm):
                mm.then_inc(w_used, 1)

            FORM = {"bc": features, "x": features, "z": tokens, "dt": tokens, "fi": features, "cb": features,
                    "cc": features, "ch": features, "q": features, "k": features, "v": tokens}

            def freed_by(kind):
                if kind in ("bc", "x"):
                    n["conv"] += 1
                    return pad_filled, n["conv"]
                if kind == "z":
                    n["z"] += 1
                    return silu_done, silu_count("z", n["z"] - 1)
                if kind == "dt":
                    n["dt"] += 1
                    return dt_biased, n["dt"]
                if kind == "fi":
                    n["mlp"] += 1
                    return relu_done, n["mlp"]
                if kind in ("q", "k", "v"):
                    n["qkv"] += 1
                    return qkv_done, n["qkv"]
                n["sc"] += 1
                c = (n["sc"] - 1) // 3 + 1
                return {"cc": sc_c, "ch": sc_prod, "cb": sc_gated}[kind], c

            def project(u, ts, bank=None, arriving=None):
                kind = units[u][0]
                if bank is None:
                    freed = freed_by(kind)
                    bank = Y[0][0] if u in extra else acc_bank(freed)
                form = tokens if kind == "fi" and units[u][2] < HEAD_UNITS else FORM[kind]
                if form is features:
                    mm = features(u, bank, ts, arriving)
                else:
                    mm = tokens(u, bank, ts, arriving, 2 * HEADS if kind == "dt" else COLS)
                if ts[-1] == NT - 1:
                    used(mm)
                return bank

            def project_half(u, part, banks):
                kind = units[u][0]
                if part == 0:
                    banks[u] = acc_bank(freed_by(kind))
                if FORM[kind] is tokens:
                    mm = tokens(u, banks[u], [part], None, COLS)
                else:
                    mm = features(u, banks[u], range(NT), None, [part])
                if part:
                    used(mm)

            def out_half(s, u, part, first):
                mm = out_part(s, u, n["opu"], first, False, [part])
                if part:
                    mm.then_inc(w_used, 1)
                    n["opu"] += 1

            def turn_x(s, t):
                for half in range(2):
                    if s:
                        pe.wait_ge(ln_out, 4 * (s - 1) + 2 * t + half + 1)
                    else:
                        pe.wait_ge(x_landed[t], 16)
                        pe.wait_ge(consts, 1)
                    bank = inner_bank(("xt", s, t, half), (xt_low, 4 * s + 2 * t + half + 1))
                    for q in range(4):
                        c = (4 * half + q) * P
                        mm = nc.tensor.transpose(bank[:, q * P:(q + 1) * P], xs[:, t, c:c + P], ident[:, :])
                    mm.then_inc(xt_turned, 1)

            def early_turn(s):
                return 0 < s < len(subs) and subs[s - 1][0] == "ffn"

            def head_units(s, us):
                banks = {}
                if s == 0:
                    turn_x(s, 0)
                for t in range(NT):
                    if s == 0 and t + 1 < NT:
                        turn_x(s, t + 1)
                    if s and (t or not early_turn(s)):
                        turn_x(s, t)
                    for i, u in enumerate(us):
                        banks[u] = project(u, [t], banks.get(u), arriving=(s, t) if i == 0 else None)

            def out_part(s, u, o, first, last, ts, ks=range(2), cs=range(2)):
                wh, wl = weights(u)
                pe.wait_ge(op_high, o + 1)
                pe.wait_ge(op_low, o + 1)
                for t in ts:
                    if first and s:
                        pe.wait_ge(y_free, 2 * (s - 1) + t + 1)
                    for k in ks:
                        for low, w in ((0, wh), (0, wl), (1, wh)):
                            for c in cs:
                                mm = nc.tensor.matmul(Y[t][c][:, :], opT[:, o % ACTS, low, k, t * P:(t + 1) * P],
                                                      w[:, k * D + c * 512:k * D + (c + 1) * 512],
                                                      start=(first and k == 0 and low == 0 and w is wh),
                                                      stop=(last and k == 1 and low == 1))
                return mm

            def out_unit(s, u, first=False, between=None):
                o = n["opu"]
                n["opu"] += 1
                if between:
                    out_part(s, u, o, first, False, [0])
                    out_part(s, u, o, first, False, [1], [0])
                    between()
                    out_part(s, u, o, first, False, [1], [1]).then_inc(w_used, 1)
                else:
                    out_part(s, u, o, first, False, range(NT)).then_inc(w_used, 1)

            def tail(s, us, first=False):
                o = n["opu"]
                n["opu"] += len(us)
                for t in range(NT):
                    for i, u in enumerate(us):
                        if i < len(us) - 1:
                            mm = out_part(s, u, o + i, first and i == 0, False, [t])
                        else:
                            out_part(s, u, o + i, first and i == 0, True, [t], cs=[0]).then_inc(y_ready, 1)
                            mm = out_part(s, u, o + i, first and i == 0, True, [t], cs=[1])
                        if t == NT - 1:
                            mm.then_inc(w_used, 1)
                        if t == NT - 1 and early_turn(s + 1) and i == len(us) - 2:
                            turn_x(s + 1, 0)
                    if t == 0:
                        mm.then_inc(y_ready, 1)

            def turn_parameters():
                for n_dmas, landed in zip(n_par_dmas, par_landed):
                    pe.wait_ge(landed, 16 * n_dmas)
                pe.wait_ge(consts, 2)
                for j in range(n_ssd):
                    bank = inner_bank(("par", j), (par_done, 2 * (j + 1)))
                    for q in range(TAPS + 2):
                        rows = CT if q <= TAPS else DI // P
                        mm = nc.tensor.transpose(bank[:, q * CT:q * CT + rows], ssd_rows[0:rows, j, q, :], ident[0:rows, 0:rows])
                    mm.then_inc(par_turned, 1)
                bank = inner_bank(("par", n_ssd), (par_done, 2 * n_ssd + 1))
                for q in range(SC_TAPS):
                    mm = nc.tensor.transpose(bank[:, q * KT:(q + 1) * KT], sc_rows[:, q, :], ident[0:KT, 0:KT])
                mm.then_inc(par_turned, 1)

            for s, (kind, j, names) in enumerate(subs):
                if kind == "ffn":
                    last = FFN // COLS - 1
                    head_units(s, [names[("fi", b)] for b in range(HEAD_UNITS)])
                    for b in range(HEAD_UNITS, last + 1):
                        project(names[("fi", b)], range(NT))
                        for q in {HEAD_UNITS: range(HEAD_UNITS - 1), HEAD_UNITS + 1: [HEAD_UNITS - 1]}.get(b, []):
                            o = n["op"] + q
                            pe.wait_ge(square_done, 16 * (s // 2) + q + 1)
                            bank = inner_bank(("op", o), (op_low, o + 1))
                            for c in range(2):
                                for t in range(NT):
                                    mm = nc.tensor.transpose(bank[:, c * SEQ + t * P:c * SEQ + (t + 1) * P],
                                                             conv[:, o % 2, t, c * P:(c + 1) * P], ident[:, :])
                            mm.then_inc(op_turned, 1)
                        if b == MLP_LAG:
                            pe.wait_ge(relu_done, 16 * (s // 2) + HEAD_UNITS)
                        if b >= MLP_LAG:
                            out_unit(s, names[("fo", b - MLP_LAG)], first=(b == MLP_LAG))
                    tail(s, [names[("fo", last + 1 - q)] for q in range(MLP_LAG, 0, -1)])
                elif kind == "ssd":
                    n0 = n["grp"]
                    n["grp"] += G
                    head_units(s, [names[("z", 0)], names[("dt", 0)]])
                    if s == 0:
                        turn_parameters()

                    def cumsum():
                        pe.wait_ge(a_steps, n0 // G + 1)
                        bank = inner_bank(("cs", j), (ncs_done, n0 // G + 1))
                        a = dtt[:, 5, :, :]
                        H = HEADS
                        for t, c, terms in ((0, 0, ((prefix, 0),)), (0, H, ((suffix, 0), (ones, 1))),
                                            (1, 0, ((ones, 0), (prefix, 1))), (1, H, ((suffix, 1),))):
                            for i, (m, src) in enumerate(terms):
                                mm = nc.tensor.matmul(bank[:, t * 2 * H + c:t * 2 * H + c + H], m[:, :], a[:, src, c:c + H],
                                                      start=(i == 0), stop=(i == len(terms) - 1))
                        mm.then_inc(cs_acc, 1)

                    def cumsum_rows():
                        pe.wait_ge(cs_copied, n0 // G + 1)
                        bank = inner_bank(("cs_rows", j), (cs_rows, n0 // G + 1))
                        for t in range(NT):
                            mm = nc.tensor.transpose(bank[0:2 * HEADS, t * P:(t + 1) * P], cs[:, t, :], ident[:, :])
                        mm.then_inc(cs_turned, 1)

                    def turn_xs(g):
                        m = n0 + g
                        pe.wait_ge(silu_done, silu_count("x", m))
                        bank = inner_bank(("xs", m), (xs_copied, m + 1))
                        for t in range(NT):
                            for c in range(2):
                                mm = nc.tensor.transpose(bank[:, t * GW + c * P:t * GW + (c + 1) * P],
                                                         xsT[:, m % 2, c, t * P:(t + 1) * P], ident[:, :])
                        mm.then_inc(xs_turned, 1)

                    def state_products(g):
                        m = n0 + g
                        pe.wait_ge(silu_done, silu_count("bc", m))
                        bank = inner_bank(("cb", m), (g_done, m + 1))
                        bc = tri_a[:, m % 2, :]
                        for t in range(NT):
                            mm = nc.tensor.matmul(bank[:, t * SEQ:(t + 1) * SEQ], bc[:, t * P:(t + 1) * P],
                                                  bc[:, SEQ:2 * SEQ], start=True, stop=True)
                        mm.then_inc(cb_ready, 1)

                    def scan(g):
                        m = n0 + g
                        pe.wait_ge(g_done, m + 1)
                        pe.wait_ge(xs_scaled, m + 1)
                        bank = inner_bank(("yg", m), (y_added, m + 1))
                        for h in range(HPG):
                            e = E[:, m % 2, h * E_HEAD:(h + 1) * E_HEAD]
                            c0, c1 = h * HD, GW + h * HD
                            for t, terms in ((0, ((0, xs_fwd, c0), (256, xs_bwd, c0), (384, xs_bwd, c1))),
                                             (1, ((P, xs_fwd, c0), (640, xs_fwd, c1), (384 + P, xs_bwd, c1)))):
                                for q, (c, v, cv) in enumerate(terms):
                                    mm = nc.tensor.matmul(bank[:, t * GW + h * HD:t * GW + (h + 1) * HD],
                                                          e[:, c:c + P], v[:, cv:cv + HD], start=(q == 0), stop=(q == 2))
                        mm.then_inc(yg_ready, 1)

                    def turn_gated(g):
                        m, o = n0 + g, n["op"] + g
                        pe.wait_ge(scaled, m + 1)
                        bank = inner_bank(("op", o), (op_low, o + 1))
                        for c in range(2):
                            for t in range(NT):
                                mm = nc.tensor.transpose(bank[:, c * SEQ + t * P:c * SEQ + (t + 1) * P],
                                                         gate[:, t * GW + c * P:t * GW + (c + 1) * P], ident[:, :])
                        mm.then_inc(op_turned, 1)

                    project(names[("bc", 0)], range(NT))
                    cumsum()
                    cumsum_rows()
                    project(names[("x", 0)], range(NT))
                    for i in range(1, G - 1):
                        project(names[("z", i)], range(NT))
                        if i <= 2:
                            project(names[("bc", i)], range(NT))
                        turn_xs(i - 1)
                        if i >= 2:
                            scan(i - 2)
                        state_products(i - 1)
                        if i > 2:
                            project(names[("bc", i)], range(NT))
                        if i > 2:
                            turn_gated(i - 2)
                        project(names[("x", i)], range(NT))
                        if i == 2:
                            turn_gated(i - 2)
                        if i >= 2:
                            out_unit(s, names[("so", i - 2)], first=(i == 2))
                    project(names[("bc", G - 1)], range(NT))
                    turn_xs(G - 2)
                    scan(G - 3)
                    state_products(G - 2)
                    project(names[("x", G - 1)], range(NT))
                    turn_gated(G - 3)
                    project(names[("z", G - 1)], range(NT))
                    scan(G - 2)
                    turn_xs(G - 1)
                    out_unit(s, names[("so", G - 3)], between=lambda: state_products(G - 1))
                    turn_gated(G - 2)
                    scan(G - 1)
                    out_unit(s, names[("so", G - 2)], between=lambda: turn_gated(G - 1))
                    tail(s, [names[("so", G - 1)]])
                    n["op"] += G
                elif kind == "conv":
                    head_units(s, [])
                    for b in range(5):
                        if b < 4:
                            project(names[("cc", b)], range(NT), arriving=None if b else (s, NT - 1))
                            project(names[("ch", b)], range(NT))
                            project(names[("cb", b)], range(NT))
                        if 1 <= b < 3:
                            out_unit(s, names[("co", b - 1)], first=(b == 1))
                    tail(s, [names[("co", 2)], names[("co", 3)]])
                else:
                    head_units(s, [names[("v", 0)]])

                    def scores(h):
                        blk, hh = h // BLOCK_HEADS, h % BLOCK_HEADS
                        pe.wait_ge(qkv_done, 3 * blk + 3)
                        bank = inner_bank(("s", h), (s_biased, h + 1))
                        rows, c = slice(64 * (hh % 2), 64 * (hh % 2) + 64), (hh // 2) * SEQ
                        for t in range(NT):
                            mm = nc.tensor.matmul(bank[:, t * SEQ:(t + 1) * SEQ],
                                                  tri_a[rows, blk % 3, c + t * P:c + (t + 1) * P],
                                                  tri_b[rows, blk % 3, c:c + SEQ], start=True, stop=True)
                        mm.then_inc(s_ready, 1)

                    def turn_probs(h):
                        pe.wait_ge(p_done, h + 1)
                        bank = inner_bank(("pt", h), (pt_done, h + 1))
                        for k in range(NT):
                            for t in range(NT):
                                mm = nc.tensor.transpose(bank[:, k * SEQ + t * P:k * SEQ + (t + 1) * P],
                                                         prob_b[h % 2][:, t * SEQ + k * P:t * SEQ + (k + 1) * P], ident[:, :])
                        mm.then_inc(pt_ready, 1)

                    def mix_values(h):
                        blk, hh = h // BLOCK_HEADS, h % BLOCK_HEADS
                        pe.wait_ge(pt_done, h + 1)
                        bank = inner_bank(("o", h), (o_done, h + 1))
                        for t in range(NT):
                            for k in range(NT):
                                mm = nc.tensor.matmul(bank[:, t * NAD:(t + 1) * NAD],
                                                      probT_b[h % 2][:, k * SEQ + t * P:k * SEQ + (t + 1) * P],
                                                      tri_c[:, blk % 3, k * COLS + hh * NAD:k * COLS + (hh + 1) * NAD],
                                                      start=(k == 0), stop=(k == NT - 1))
                        mm.then_inc(o_ready, 1)

                    def turn_out(blk):
                        o = n["op"]
                        n["op"] += 1
                        pe.wait_ge(o_done, BLOCK_HEADS * (blk + 1))
                        bank = inner_bank(("op", o), (op_low, o + 1))
                        for c in range(2):
                            for t in range(NT):
                                mm = nc.tensor.transpose(bank[:, c * SEQ + t * P:c * SEQ + (t + 1) * P],
                                                         o_b[blk % 2][:, t * COLS + c * P:t * COLS + (c + 1) * P], ident[:, :])
                        mm.then_inc(op_turned, 1)

                    halves = ([(what, b, part) for b in range(1, 4) for what in "vqk" for part in range(2)]
                              + [("no", b, part) for b in range(3) for part in range(2)])
                    share = [3, 1, 2, 1] + 2 * [2, 1, 2, 1] + [2, 1, 1, 1]
                    banks = {}
                    for b in range(6):
                        for k in range(4):
                            h = 4 * (b - 1) + k
                            if 0 <= h < NAH:
                                scores(h)
                                for _ in range(share[h]):
                                    what, blk, part = halves.pop(0)
                                    if what == "no":
                                        out_half(s, names[(what, blk)], part, blk == 0)
                                    else:
                                        project_half(names[(what, blk)], part, banks)
                            elif b == 0 and 1 <= k < 3:
                                project(names[("vqk"[k], b)], range(NT))
                            if 1 <= h <= NAH:
                                mix_values(h - 1)
                            if 0 <= h < NAH:
                                turn_probs(h)
                            if k == 1 and b >= 2:
                                turn_out(b - 2)
                    tail(s, [names[("no", 3)]])
                if kind in ("ffn", "conv"):
                    n["op"] += FFN // COLS if kind == "ffn" else 4

        def reversed_rows(bank):
            ap = bank[:, :]
            return bass.AP(ap.tensor, ap.offset + GRID_W - 1, [list(ap.ap[0]), [GRID_W, 2 * ROWS], [-1, GRID_W]])

        def grid_rows(ap):
            return ap.rearrange("p a b -> p (a b)").rearrange("p (a c) -> p a c", c=GRID_W)

        def tap(j, q, ct):
            return ssd_par[:, j, q, ct:ct + 1]

        def channel_tiles(kind, g):
            return (2 * g, 2 * g + 1) if kind == "x" else (2 * G + g, 3 * G + g)

        @block.scalar
        def _(act):
            load_parameters(act, 0, par_landed[0])
            n = dict.fromkeys(["split", "step", "op", "turned", "grp", "conv", "th", "mlp"], 0)

            def split_to(last):
                while n["split"] <= min(last, len(units) - 1):
                    u = n["split"]
                    n["split"] += 1
                    _, k, c = weight_parts(u)
                    act.wait_ge(raw_landed[u % RAW], 32 * (u // RAW + 1))
                    if u >= SPLIT:
                        act.wait_ge(w_used, u - SPLIT + 1)
                    nc.scalar.activation(w_high[:, u % SPLIT, 0:k * c], raw[:, u % RAW, 0:k * c],
                                         ACT.Copy).then_inc(w_high_done, 1)

            def result(u):
                split_to(u + 3)
                act.wait_ge(w_used, u + 1)
                return acc_of[u]

            def operand(o):
                if o >= ACTS:
                    act.wait_ge(w_used, out_units[o - ACTS] + 1)
                return opT[:, o % ACTS, 0, :, :]

            def operand_high(o, ready, count):
                act.wait_ge(ready, count)
                nc.scalar.activation(operand(o), conv[:, o % 2, :, :], ACT.Copy).then_inc(op_high, 1)

            for s, (kind, j, names) in enumerate(subs):
                for t in range(NT):
                    if s:
                        split_to(ahead_of_norm(s - 1, t))
                        split_to(last_unit[s - 1] + 1)
                    for half in range(2):
                        act.wait_ge(xt_turned, 4 * s + 2 * t + half + 1)
                        bank = inner_of[("xt", s, t, half)]
                        nc.scalar.activation(xT[:, 4 * half:4 * half + 4, 0, t * P:(t + 1) * P],
                                             bank[:, :].rearrange("p (k c) -> p k c", k=4), ACT.Copy).then_inc(xt_high, 1)
                    if not s:
                        split_to(t)
                if kind == "ffn":
                    blocks = FFN // COLS
                    for b in range(blocks + 1):
                        if b < blocks:
                            o = n["op"] + b
                            bank = result(names[("fi", b)])
                            if o >= 2:
                                act.wait_ge(op_low, o - 1)
                            nc.scalar.activation(conv[:, o % 2, :, :], views(bank[:, :]), ACT.Relu).then_inc(relu_done, 1)
                        if b >= 1:
                            split_to(names[("fi", min(b + 1, blocks - 1))] + 2)
                            m = n["mlp"]
                            n["mlp"] += 1
                            o = n["op"] + b - 1
                            if b > HEAD_UNITS:
                                operand_high(o, square_done, m + 1)
                            else:
                                n["turned"] += 1
                                act.wait_ge(op_turned, n["turned"])
                                nc.scalar.activation(operand(o), views(inner_of[("op", o)][:, :]), ACT.Copy).then_inc(op_high, 1)
                    n["op"] += blocks
                elif kind == "ssd":
                    n0 = n["grp"]
                    n["grp"] += G
                    mixer = n0 // G

                    def start_conv(kind, g):
                        c = n["conv"]
                        n["conv"] += 1
                        bank = result(names[(kind, g)])
                        if c >= 2:
                            act.wait_ge(taps_done, 2 * (c - 1))
                        nc.scalar.activation(pad[:, c % 2, :, 2:2 + SEQ], views(bank[:, :]), ACT.Copy).then_inc(pad_filled, 1)
                        act.wait_ge(pad_filled, c + 1)
                        if c >= 2:
                            act.wait_ge(silu_done, silu_count("x" if c % 2 else "bc", (c - 2) // 2))
                        for q, ct in enumerate(channel_tiles(kind, g)):
                            nc.scalar.activation(conv[:, c % 2, q, :], pad[:, c % 2, q, 0:SEQ], ACT.Identity,
                                                 bias=tap(j, TAPS, ct), scale=tap(j, 0, ct)).then_inc(first_tap, 1)

                    def tanh_of(src, scale):
                        m = n["th"]
                        n["th"] += 1
                        if m >= 2:
                            act.wait_ge(silu_done, m - 1)
                        nc.scalar.activation(th[:, m % 2, :], src, ACT.Tanh, scale=scale).then_inc(tanh_done, 1)

                    def conv_tanh():
                        c = n["conv"] - 1
                        act.wait_ge(taps_done, 2 * (c + 1))
                        tanh_of(conv[:, c % 2, :, :].rearrange("p a b -> p (a b)"), 1.0)

                    def decays(g, heads):
                        m = n0 + g
                        act.wait_ge(e_masked, m + 1)
                        for h in heads:
                            for q, (off, width) in enumerate(E_PART):
                                col = (HEADS if q in (1, 2) else 0) + g * HPG + h
                                e = E[:, m % 2, h * E_HEAD + off:h * E_HEAD + off + width]
                                ins = nc.scalar.activation(e, e, ACT.Exp, bias=ncs[:, q // 2, col:col + 1])
                        ins.then_inc(e_exp, 1)

                    early, late = range(HPG // 2), range(HPG // 2, HPG)

                    def copy_xs(g):
                        m = n0 + g
                        act.wait_ge(xs_turned, m + 1)
                        if m >= 2:
                            act.wait_ge(gated, m - 1)
                        nc.scalar.activation(tri_b[:, m % 2, :], inner_of[("xs", m)][:, :], ACT.Copy).then_inc(xs_copied, 1)

                    def squares(g):
                        m = n0 + g
                        act.wait_ge(gated, m + 1)
                        if m:
                            act.wait_ge(rms_done, m)
                        for t in range(NT):
                            ins = nc.scalar.activation(sq[:, t * GW:(t + 1) * GW], gate[:, t * GW:(t + 1) * GW],
                                                       ACT.Square, accum_out=small[:, 4 + t:5 + t])
                        ins.then_inc(msq_done, 1)

                    def normalise(g):
                        act.wait_ge(rms_done, n0 + g + 1)
                        for t in range(NT):
                            v = gate[:, t * GW:(t + 1) * GW]
                            ins = nc.scalar.activation(v, v, ACT.Copy, scale=small[:, 8 + t:9 + t])
                        ins.then_inc(scaled, 1)

                    def gated_high(g):
                        o = n["op"] + g
                        n["turned"] += 1
                        act.wait_ge(op_turned, n["turned"])
                        dst = operand(o)
                        for c in range(2):
                            ins = nc.scalar.activation(dst[:, c, :], inner_of[("op", o)][:, c * SEQ:(c + 1) * SEQ],
                                                       ACT.Copy, scale=tap(j, TAPS + 1, 2 * g + c))
                        ins.then_inc(op_high, 1)

                    if s == 0:
                        split_to(3)
                        for n_dmas, landed in zip(n_par_dmas, par_landed):
                            act.wait_ge(landed, 16 * n_dmas)
                        for q in range(n_ssd):
                            ins = nc.scalar.activation(a_neg[:, q, :], a_neg[:, q, :], ACT.Exp)
                        ins.then_inc(a_done, 1)
                        act.wait_ge(par_done, 2 * n_ssd + 1)
                    def z_tanh(g):
                        bank = result(names[("z", g)])
                        tanh_of(bank[:, :], 0.5)

                    z_tanh(0)
                    split_to(names[("dt", 0)] + 3)
                    act.wait_ge(dt_biased, mixer + 1)
                    nc.scalar.activation(dtt[:, 1, :, :], dtt[:, 0, :, :], ACT.Abs).then_inc(act_step, 1)
                    n["step"] += 1
                    act.wait_ge(act_step, n["step"])
                    nc.scalar.activation(dtt[:, 2, :, :], dtt[:, 1, :, :], ACT.Exp, scale=-1.0).then_inc(dt_exp, 1)
                    split_to(names[("bc", 0)] + 3)
                    act.wait_ge(cs_copied, mixer + 1)
                    nc.scalar.activation(ncs[:, :, :], inner_of[("cs", j)][:, 0:NT * 2 * HEADS]
                                         .rearrange("p (t c) -> p t c", t=NT), ACT.Copy,
                                         scale=-1.0).then_inc(ncs_done, 1)
                    act.wait_ge(cs_rows, mixer + 1)
                    act.dma_start(rows_dram[j], csT[:, :]).then_inc(rows_stored, 16)
                    act.wait_ge(ncs_done, mixer + 1)
                    for kind_of in ("bc", "x"):
                        start_conv(kind_of, 0)
                        conv_tanh()
                    for i in range(1, G - 1):
                        z_tanh(i)
                        if i > 2:
                            copy_xs(i - 1)
                            squares(i - 2)
                            split_to(names[("bc", i)] + 3)
                            normalise(i - 2)
                        start_conv("bc", i)
                        if i > 2:
                            gated_high(i - 2)
                        else:
                            copy_xs(i - 1)
                        if i <= 2:
                            decays(i - 1, early)
                        if i == 2:
                            decays(1, late)
                        conv_tanh()
                        if i == 2:
                            squares(0)
                            normalise(0)
                            gated_high(0)
                        start_conv("x", i)
                        if i == 1:
                            decays(0, late)
                        if i > 1:
                            decays(i, early)
                        conv_tanh()
                        if i > 1:
                            decays(i, late)
                    start_conv("bc", G - 1)
                    copy_xs(G - 2)
                    conv_tanh()
                    squares(G - 3)
                    normalise(G - 3)
                    start_conv("x", G - 1)
                    gated_high(G - 3)
                    conv_tanh()
                    decays(G - 1, early)
                    z_tanh(G - 1)
                    decays(G - 1, late)
                    copy_xs(G - 1)
                    squares(G - 2)
                    normalise(G - 2)
                    gated_high(G - 2)
                    split_to(names[("so", G - 1)] + 2)
                    squares(G - 1)
                    normalise(G - 1)
                    gated_high(G - 1)
                    n["op"] += G
                elif kind == "conv":
                    for b in range(5):
                        if b < 4:
                            bank = result(names[("cc", b)])
                            if b >= 2:
                                act.wait_ge(sc_prod, b - 1)
                            nc.scalar.activation(th[:, b % 2, :], bank[:, :], ACT.Copy).then_inc(sc_c, 1)
                        if b >= 1:
                            split_to(names[("cb", b - 1)] + 3)
                            operand_high(n["op"], sc_gated, b)
                            n["op"] += 1
                else:
                    def keep_qkv(k, b):
                        bank = result(names[("vqk"[k], b)])
                        if b == 3:
                            act.wait_ge(o_ready, BLOCK_HEADS)
                        dst = (tri_c, tri_a, tri_b)[k]
                        src = reversed_rows(bank) if k == 1 else bank[:, :]
                        out = dst[:, b % 3, :].rearrange("p (a c) -> p a c", c=GRID_W) if k == 1 else dst[:, b % 3, :]
                        nc.scalar.activation(out, src, ACT.Copy).then_inc(qkv_done, 1)

                    def scale_out(h):
                        blk, hh = h // BLOCK_HEADS, h % BLOCK_HEADS
                        act.wait_ge(o_ready, h + 1)
                        act.wait_ge(p_scale, h + 1)
                        if blk >= 2 and hh == 0:
                            act.wait_ge(op_turned, n["turned"] - (1 if n["turned"] > base + blk - 1 else 0))
                        for t in range(NT):
                            c = t * COLS + hh * NAD
                            ins = nc.scalar.activation(o_b[blk % 2][:, c:c + NAD], inner_of[("o", h)][:, t * NAD:(t + 1) * NAD],
                                                       ACT.Copy, scale=att[:, h % 2, 6 + t:7 + t])
                        ins.then_inc(o_done, 1)

                    base = n["turned"]
                    for b in range(6):
                        for k in range(4):
                            h = 4 * (b - 1) + k
                            if 0 <= h < NAH:
                                act.wait_ge(s_max, h + 1)
                                for t in range(NT):
                                    v = prob_b[h % 2][:, t * SEQ:(t + 1) * SEQ]
                                    ins = nc.scalar.activation(v, v, ACT.Exp, bias=att[:, h % 2, 2 + t:3 + t],
                                                               accum_out=att[:, h % 2, 4 + t:5 + t])
                                ins.then_inc(p_done, 1)
                            if k < 3 and b < 4:
                                keep_qkv(k, b)
                            if b == 4 and k >= 2:
                                split_to(names[("no", 3)] + k - 2)
                            if 1 <= h <= NAH:
                                scale_out(h - 1)
                            if 0 <= h < NAH:
                                act.wait_ge(pt_ready, h + 1)
                                nc.scalar.activation(probT_b[h % 2], inner_of[("pt", h)][:, :], ACT.Copy).then_inc(pt_done, 1)
                            if k == 1 and b >= 2:
                                o = n["op"]
                                n["op"] += 1
                                n["turned"] += 1
                                act.wait_ge(op_turned, n["turned"])
                                nc.scalar.activation(grid_rows(operand(o)), reversed_rows(inner_of[("op", o)]),
                                                     ACT.Copy).then_inc(op_high, 1)

            split_to(len(units) - 1)

        @block.vector
        def _(dve):
            n = dict.fromkeys(["split", "step", "op", "turned", "grp", "conv", "th", "mlp"], 0)
            V = nc.vector

            def step(ins):
                ins.then_inc(dve_step, 1)
                n["step"] += 1
                return n["step"]

            def after(count):
                dve.wait_ge(dve_step, count)

            def chain(ins):
                after(step(ins))

            def split_to(last):
                while n["split"] <= min(last, len(units) - 1):
                    u = n["split"]
                    n["split"] += 1
                    _, k, c = weight_parts(u)
                    dve.wait_ge(raw_landed[u % RAW], 32 * (u // RAW + 1))
                    dve.wait_ge(w_high_done, u + 1)
                    if u >= SPLIT:
                        dve.wait_ge(w_used, u - SPLIT + 1)
                    V.tensor_tensor(w_low[:, u % SPLIT, 0:k * c], raw[:, u % RAW, 0:k * c],
                                    f(w_high[:, u % SPLIT, 0:k * c]), ALU.subtract).then_inc(w_low_done, 1)

            def result(u):
                split_to(u + 3)
                dve.wait_ge(w_used, u + 1)
                return acc_of[u]

            def operand(o):
                if o >= ACTS:
                    dve.wait_ge(w_used, out_units[o - ACTS] + 1)
                return opT[:, o % ACTS, 1, :, :], f(opT[:, o % ACTS, 0, :, :])

            def operand_low(o, src):
                dve.wait_ge(op_high, o + 1)
                low, high = operand(o)
                V.tensor_tensor(low, src, high, ALU.subtract).then_inc(op_low, 1)

            def norm(s, t):
                split_to(ahead_of_norm(s, t))
                dve.wait_ge(y_ready, 3 * s + 1 + 2 * t)
                halves = [xs[:, t, c * 512:(c + 1) * 512] for c in range(2)]
                a = step(V.scalar_tensor_tensor(out=halves[0], in0=halves[0], scalar=ALPHA, in1=Y[t][0][:, :],
                                                op0=ALU.mult, op1=ALU.add))
                after(a)
                V.bn_stats(stats[:, 0, :], halves[0])
                if t == 0:
                    dve.wait_ge(y_ready, 3 * s + 2)
                else:
                    dve.wait_ge(w_used, last_unit[s] + 1)
                V.scalar_tensor_tensor(out=halves[1], in0=halves[1], scalar=ALPHA, in1=Y[t][1][:, :],
                                       op0=ALU.mult, op1=ALU.add).then_inc(y_free, 1)
                dve.wait_ge(y_free, 2 * s + t + 1)
                chain(V.bn_stats(stats[:, 1, :], halves[1]))
                chain(V.bn_aggr(mv[:, :], stats[:, :, :]))
                V.tensor_scalar(small[:, t:t + 1], mv[:, 1:2], EPS, None, ALU.add).then_inc(var_done, 1)
                dve.wait_ge(gb_landed, 32 * (s + 1))
                cents = []
                for c in range(2):
                    cents.append(step(V.scalar_tensor_tensor(out=halves[c], in0=halves[c], scalar=mv[:, 0:1],
                                                             in1=gb[:, 0, c * 512:(c + 1) * 512],
                                                             op0=ALU.subtract, op1=ALU.mult)))
                dve.wait_ge(rstd_done, 2 * s + t + 1)
                for c in range(2):
                    after(cents[c])
                    V.scalar_tensor_tensor(out=halves[c], in0=halves[c], scalar=small[:, 2 + t:3 + t],
                                           in1=gb[:, 1, c * 512:(c + 1) * 512],
                                           op0=ALU.mult, op1=ALU.add).then_inc(ln_out, 1)

            for s, (kind, j, names) in enumerate(subs):
                for t in range(NT):
                    if s:
                        norm(s - 1, t)
                        split_to(last_unit[s - 1] + 1)
                    for half in range(2):
                        m = 4 * s + 2 * t + half + 1
                        dve.wait_ge(xt_high, m)
                        dst = xT[:, 4 * half:4 * half + 4, :, t * P:(t + 1) * P]
                        V.tensor_tensor(dst[:, :, 1, :], inner_of[("xt", s, t, half)][:, :].rearrange("p (k c) -> p k c", k=4),
                                        f(dst[:, :, 0, :]), ALU.subtract).then_inc(xt_low, 1)
                    if not s:
                        split_to(t)
                if kind == "ffn":
                    def turned_low(o):
                        dve.wait_ge(op_turned, n["turned"] + 1)
                        n["turned"] += 1
                        operand_low(o, views(inner_of[("op", o)][:, :]))

                    for b in range(FFN // COLS):
                        o = n["op"]
                        n["op"] += 1
                        m = n["mlp"]
                        n["mlp"] += 1
                        result(names[("fi", b)])
                        dve.wait_ge(relu_done, m + 1)
                        V.tensor_tensor(conv[:, o % 2, :, :], conv[:, o % 2, :, :], conv[:, o % 2, :, :],
                                        ALU.mult).then_inc(square_done, 1)
                        if b + 1 < FFN // COLS:
                            split_to(names[("fi", b + 1)] + 2)
                        if 1 <= b <= HEAD_UNITS:
                            turned_low(o - 1)
                        if b >= HEAD_UNITS:
                            dve.wait_ge(square_done, m + 1)
                            operand_low(o, conv[:, o % 2, :, :])
                elif kind == "ssd":
                    n0 = n["grp"]
                    n["grp"] += G
                    mixer = n0 // G

                    def time_constants():
                        bank = result(names[("dt", 0)])
                        cols = 2 * HEADS
                        V.tensor_tensor(dtt[:, 0, :, :], bank[:, 0:NT * cols].rearrange("p (t c) -> p t c", t=NT),
                                        spread(dt_bias[:, j, :], [[0, NT], [1, cols]]), ALU.add).then_inc(dt_biased, 1)
                        dve.wait_ge(dt_exp, mixer + 1)
                        v, w1, e, r, r2, a = (dtt[:, q, :, :] for q in range(6))
                        chain(V.tensor_scalar(w1, e, 2.0, None, ALU.add))
                        chain(V.reciprocal(w1, w1))
                        chain(V.tensor_tensor(r, e, w1, ALU.mult))
                        chain(V.tensor_tensor(r2, r, r, ALU.mult))
                        chain(V.tensor_scalar(e, r2, 1.0 / 15, None, ALU.mult))
                        for q in (13, 11, 9, 7, 5, 3):
                            chain(V.scalar_tensor_tensor(out=e, in0=e, scalar=1.0 / q, in1=r2, op0=ALU.add, op1=ALU.mult))
                        chain(V.scalar_tensor_tensor(out=e, in0=e, scalar=1.0, in1=r, op0=ALU.add, op1=ALU.mult))
                        chain(V.tensor_scalar(w1, v, 0.0, None, ALU.max))
                        chain(V.scalar_tensor_tensor(out=dts[:, :, :], in0=e, scalar=2.0, in1=w1, op0=ALU.mult, op1=ALU.add))
                        V.scalar_tensor_tensor(out=a, in0=dts[:, :, :], scalar=-1.0,
                                               in1=spread(a_neg[:, j, :], [[0, NT], [1, cols]]),
                                               op0=ALU.mult, op1=ALU.mult).then_inc(a_steps, 1)

                    def taps(kind, g):
                        c = n["conv"]
                        n["conv"] += 1
                        split_to(names[(kind, g)] + 3)
                        dve.wait_ge(first_tap, 2 * (c + 1))
                        done = [0, 0]
                        for q in range(1, TAPS):
                            for i, ct in enumerate(channel_tiles(kind, g)):
                                if q > 1:
                                    after(done[i])
                                y = conv[:, c % 2, i, :]
                                ins = V.scalar_tensor_tensor(out=y, in0=pad[:, c % 2, i, q:q + SEQ], scalar=tap(j, q, ct),
                                                             in1=y, op0=ALU.mult, op1=ALU.add)
                                if q < TAPS - 1:
                                    done[i] = step(ins)
                                else:
                                    ins.then_inc(taps_done, 1)
                        return conv[:, c % 2, :, :].rearrange("p a b -> p (a b)")

                    def silu(dst, half_y):
                        m = n["th"]
                        n["th"] += 1
                        dve.wait_ge(tanh_done, m + 1)
                        V.scalar_tensor_tensor(out=dst, in0=th[:, m % 2, :], scalar=1.0, in1=half_y,
                                               op0=ALU.add, op1=ALU.mult).then_inc(silu_done, 1)

                    def gated_low(g):
                        o = n["op"] + g
                        dve.wait_ge(op_high, o + 1)
                        low, high = operand(o)
                        for c in range(2):
                            ins = V.scalar_tensor_tensor(out=low[:, c, :], in0=inner_of[("op", o)][:, c * SEQ:(c + 1) * SEQ],
                                                         scalar=tap(j, TAPS + 1, 2 * g + c), in1=high[:, c, :],
                                                         op0=ALU.mult, op1=ALU.subtract)
                        ins.then_inc(op_low, 1)

                    def decayed_products(g):
                        m = n0 + g
                        dve.wait_ge(cb_ready, m + 1)
                        dve.wait_ge(e_exp, 2 * (m + 1))
                        slot = E[:, m % 2, :].rearrange("p (h e) -> p h e", h=HPG)
                        for q, (off, width) in enumerate(E_PART):
                            l0 = (q // 2) * SEQ + (P if q == 3 else 0)
                            v = slot[:, :, off:off + width]
                            ins = V.tensor_tensor(v, v, spread(inner_of[("cb", m)][:, l0:l0 + width],
                                                               [[0, HPG], [1, width]]), ALU.mult)
                        ins.then_inc(g_done, 1)

                    def gate_scan(g):
                        m = n0 + g
                        dve.wait_ge(xs_skip, m + 1)
                        if g:
                            dve.wait_ge(op_turned, n["turned"] + 1)
                            n["turned"] += 1
                        dve.wait_ge(yg_ready, m + 1)
                        V.tensor_tensor(gate[:, :], tri_b[:, m % 2, :], inner_of[("yg", m)][:, :], ALU.add).then_inc(y_added, 1)
                        dve.wait_ge(y_added, m + 1)
                        V.scalar_tensor_tensor(out=gate[:, :], in0=gate[:, :], scalar=0.5, in1=tri_c[:, m % 3, :],
                                               op0=ALU.mult, op1=ALU.mult).then_inc(gated, 1)

                    if s == 0:
                        split_to(3)
                        for q in range(n_ssd):
                            dve.wait_ge(par_turned, q + 1)
                            bank = inner_of[("par", q)]
                            V.tensor_scalar(ssd_par[:, q, 0:TAPS + 1, :], bank[:, 0:(TAPS + 1) * CT]
                                            .rearrange("p (a b) -> p a b", b=CT), 0.5, None, ALU.mult).then_inc(par_done, 1)
                            V.tensor_copy(ssd_par[:, q, TAPS + 1, 0:DI // P],
                                          bank[:, (TAPS + 1) * CT:(TAPS + 1) * CT + DI // P]).then_inc(par_done, 1)
                        dve.wait_ge(par_turned, n_ssd + 1)
                        V.tensor_copy(sc_par[:, :, :], inner_of[("par", n_ssd)][:, 0:SC_TAPS * KT]
                                      .rearrange("p (a b) -> p a b", b=KT)).then_inc(par_done, 1)
                        dve.wait_ge(par_done, 2 * n_ssd + 1)
                        dve.wait_ge(a_done, 1)
                    def silu_z(g):
                        m = n0 + g
                        bank = result(names[("z", g)])
                        if m >= 3:
                            dve.wait_ge(gated, m - 2)
                        silu(tri_c[:, m % 3, :], bank[:, :])

                    def silu_bc(g, y):
                        m = n0 + g
                        if m >= 2:
                            dve.wait_ge(cb_ready, m - 1)
                        silu(tri_a[:, m % 2, :], y)

                    def silu_x(g, y):
                        m = n0 + g
                        if m >= 2:
                            dve.wait_ge(xs_turned, m - 1)
                        silu(xsT[:, m % 2, :, :].rearrange("p a b -> p (a b)"), y)

                    silu_z(0)
                    time_constants()
                    split_to(names[("bc", 0)] + 3)
                    dve.wait_ge(cs_acc, mixer + 1)
                    V.tensor_copy(cs[:, :, :], inner_of[("cs", j)][:, 0:NT * 2 * HEADS]
                                  .rearrange("p (t c) -> p t c", t=NT)).then_inc(cs_copied, 1)
                    dve.wait_ge(cs_turned, mixer + 1)
                    V.tensor_copy(csT[:, :], inner_of[("cs_rows", j)][0:2 * HEADS, 0:SEQ]).then_inc(cs_rows, 1)
                    silu_bc(0, taps("bc", 0))
                    silu_x(0, taps("x", 0))
                    for i in range(1, G - 1):
                        silu_z(i)
                        if i > 2:
                            gate_scan(i - 2)
                            decayed_products(i - 1)
                        y = taps("bc", i)
                        if i > 2:
                            gated_low(i - 2)
                        silu_bc(i, y)
                        if i == 2:
                            gate_scan(0)
                            decayed_products(1)
                            gated_low(0)
                        silu_x(i, taps("x", i))
                        if i == 1:
                            decayed_products(0)
                    silu_bc(G - 1, taps("bc", G - 1))
                    gate_scan(G - 3)
                    decayed_products(G - 2)
                    y = taps("x", G - 1)
                    gated_low(G - 3)
                    silu_x(G - 1, y)
                    silu_z(G - 1)
                    gate_scan(G - 2)
                    decayed_products(G - 1)
                    gated_low(G - 2)
                    split_to(names[("so", G - 1)] + 2)
                    gate_scan(G - 1)
                    gated_low(G - 1)
                    n["op"] += G
                    n["turned"] += 1
                elif kind == "conv":
                    for b in range(4):
                        o = n["op"]
                        n["op"] += 1
                        bank = result(names[("ch", b)])
                        dve.wait_ge(sc_c, b + 1)
                        V.tensor_tensor(pad[:, b % 2, :, 2:2 + SEQ], views(th[:, b % 2, :]), views(bank[:, :]),
                                        ALU.mult).then_inc(sc_prod, 1)
                        dve.wait_ge(sc_prod, b + 1)
                        if o >= 2:
                            dve.wait_ge(op_high, o - 1)
                            dve.wait_ge(op_low, o - 1)
                        done = [0, 0]
                        for q in range(SC_TAPS):
                            for i in range(2):
                                ct = 2 * b + i
                                y, src, w = conv[:, o % 2, i, :], pad[:, b % 2, i, 1 + q:1 + q + SEQ], sc_par[:, q, ct:ct + 1]
                                if q:
                                    after(done[i])
                                    done[i] = step(V.scalar_tensor_tensor(out=y, in0=src, scalar=w, in1=y,
                                                                          op0=ALU.mult, op1=ALU.add))
                                else:
                                    done[i] = step(V.tensor_scalar(y, src, w, None, ALU.mult))
                        bank = result(names[("cb", b)])
                        after(done[1])
                        V.tensor_tensor(conv[:, o % 2, :, :], conv[:, o % 2, :, :], views(bank[:, :]),
                                        ALU.mult).then_inc(sc_gated, 1)
                        dve.wait_ge(sc_gated, b + 1)
                        operand_low(o, conv[:, o % 2, :, :])
                else:
                    for b in range(6):
                        for k in range(4):
                            h = 4 * (b - 1) + k
                            if 0 <= h < NAH:
                                p, st = prob_b[h % 2], att[:, h % 2, :]
                                dve.wait_ge(s_ready, h + 1)
                                dve.wait_ge(bias_masked, h + 1)
                                if h >= 2:
                                    dve.wait_ge(pt_ready, h - 1)
                                    dve.wait_ge(o_done, h - 1)
                                V.scalar_tensor_tensor(out=p, in0=inner_of[("s", h)][:, :], scalar=float(NAD) ** -0.5,
                                                       in1=bias_b[h % 4], op0=ALU.mult, op1=ALU.add).then_inc(s_biased, 1)
                                dve.wait_ge(s_biased, h + 1)
                                chain(V.tensor_reduce(st[:, 0:2], views(p), AX.X, ALU.max))
                                V.tensor_scalar(st[:, 2:4], st[:, 0:2], -1.0, None, ALU.mult).then_inc(s_max, 1)
                            if k < 3 and b < 4:
                                split_to(names[("vqk"[k], b)] + 3)
                            if b == 4 and k >= 2:
                                split_to(names[("no", 3)] + k - 2)
                            if 0 <= h < NAH:
                                dve.wait_ge(p_done, h + 1)
                                V.reciprocal(st[:, 6:8], st[:, 4:6]).then_inc(p_scale, 1)
                            if k == 1 and b >= 2:
                                o = n["op"]
                                n["op"] += 1
                                n["turned"] += 1
                                dve.wait_ge(op_high, o + 1)
                                low, high = operand(o)
                                V.tensor_tensor(grid_rows(low), reversed_rows(inner_of[("op", o)]), grid_rows(high),
                                                ALU.subtract).then_inc(op_low, 1)
            for t in range(NT):
                norm(len(subs) - 1, t)


_INS = ["x", "ln_mix_g", "ln_mix_b", "ln_ffn_g", "ln_ffn_b", "ffn_w_in", "ffn_w_out", "ssd_w_in", "ssd_conv_w",
        "ssd_conv_b", "ssd_dt_bias", "ssd_a_log", "ssd_d", "ssd_norm_w", "ssd_w_out", "sc_w_in", "sc_conv_w",
        "sc_w_out", "na_w_qkv", "na_rpb", "na_w_out"]


def kernel(**inputs):
    import numpy as np
    import concourse.bacc as bacc
    from concourse.bass_utils import run_bass_kernel_spmd

    nc = bacc.Bacc("TRN2", target_bir_lowering=False, num_devices=1)
    arrays, args = {}, []
    for name in _INS:
        a = np.ascontiguousarray(inputs[name])
        arrays[f"in_{name}"] = a
        args.append(nc.dram_tensor(f"in_{name}", a.shape, mybir.dt.from_np(a.dtype), kind="ExternalInput").ap())
    args.append(nc.dram_tensor("out_x", (1, SEQ, D), F32, kind="ExternalOutput").ap())
    build(nc, *args)
    r = run_bass_kernel_spmd(nc, [arrays], core_ids=[0])
    return r.results[0]["out_x"]
```
